# Optimizing a Trainium2 kernel written in Bass

```python
import jax, jax.numpy as jnp
from jax import lax
import numpy as np

D_MODEL = 2048
BATCH = 1
SEQ = 512
DEPTH = 1

CHUNK = 64
CONV_DIM = D_MODEL // 2
CONV_WIDTH = 31
N_Q_HEADS = 16
N_KV_HEADS = 2
HEAD_DIM = 64
Q_DIM = N_Q_HEADS * HEAD_DIM
KV_DIM = N_KV_HEADS * HEAD_DIM
WINDOW = 128
WINDOW_CHUNKS = WINDOW // CHUNK
BAND = WINDOW_CHUNKS * CHUNK
N_BRANCHES = 2
IN_DIM = 2 * CONV_DIM + Q_DIM + 2 * KV_DIM + N_BRANCHES * D_MODEL
PEER_HEADS = 8
PEER_KEY_DIM = 256
PEER_HALF = PEER_KEY_DIM // 2
N_KEYS = 128
N_EXPERTS = N_KEYS * N_KEYS
PEER_TOPK = 16
PEER_BLOCK = 128
RMS_EPS = 1e-6
LN_EPS = 1e-5
NEG_INF = -1e30

kernel_name = "hybrid_conv_swa_sink_peer_block"

def rmsnorm(x, g):
    xf = x.astype(jnp.float32)
    y = xf * lax.rsqrt(jnp.mean(xf * xf, axis=-1, keepdims=True) + RMS_EPS)
    return (y * g.astype(jnp.float32)).astype(x.dtype)

def layernorm(x, g, b):
    xf = x.astype(jnp.float32)
    mu = jnp.mean(xf, axis=-1, keepdims=True)
    var = jnp.mean(jnp.square(xf - mu), axis=-1, keepdims=True)
    y = (xf - mu) * lax.rsqrt(var + LN_EPS)
    return (y * g.astype(jnp.float32) + b.astype(jnp.float32)).astype(x.dtype)

def alibi_slopes(n_heads):
    h = np.arange(1, n_heads + 1, dtype=np.float32)
    return jnp.asarray(np.power(np.float32(2.0), -8.0 * h / n_heads).astype(np.float32))

def conformer_conv(zc, dw_w, dw_b, ln_g, ln_b, w_pw):
    a, gate = jnp.split(zc, 2, axis=-1)
    u = a * jax.nn.sigmoid(gate)
    u = lax.conv_general_dilated(
        u, dw_w[:, None, :].astype(u.dtype), window_strides=(1,),
        padding=[(CONV_WIDTH - 1, 0)],
        dimension_numbers=("NWC", "WIO", "NWC"),
        feature_group_count=CONV_DIM) + dw_b
    u = jax.nn.silu(layernorm(u, ln_g, ln_b))
    return u @ w_pw

def banded_sink_attention(q, k, v, sinks):
    B, T = q.shape[0], q.shape[1]
    nc = T // CHUNK
    G = N_Q_HEADS // N_KV_HEADS
    qc = q.reshape(B, nc, CHUNK, N_KV_HEADS, G, HEAD_DIM).astype(jnp.float32)
    pad = ((0, 0), (WINDOW_CHUNKS - 1, 0), (0, 0), (0, 0), (0, 0))
    kc = jnp.pad(k.reshape(B, nc, CHUNK, N_KV_HEADS, HEAD_DIM), pad)
    vc = jnp.pad(v.reshape(B, nc, CHUNK, N_KV_HEADS, HEAD_DIM), pad)
    kb = jnp.concatenate([kc[:, j:j + nc] for j in range(WINDOW_CHUNKS)], axis=2)
    vb = jnp.concatenate([vc[:, j:j + nc] for j in range(WINDOW_CHUNKS)], axis=2)
    scores = jnp.einsum("bcqkgd,bcskd->bckgqs", qc, kb.astype(jnp.float32)) * (HEAD_DIM ** -0.5)
    qi = jnp.arange(CHUNK)[:, None]
    si = jnp.arange(BAND)[None, :]
    dist = jnp.abs((WINDOW_CHUNKS - 1) * CHUNK + qi - si).astype(jnp.float32)
    slopes = alibi_slopes(N_Q_HEADS).reshape(N_KV_HEADS, G)
    scores = scores - slopes[:, :, None, None] * dist
    key_chunk = jnp.arange(nc)[:, None] - (WINDOW_CHUNKS - 1) + si // CHUNK
    valid = (key_chunk >= 0)[None, :, None, None, None, :]
    scores = jnp.where(valid, scores, NEG_INF)
    sink = sinks.astype(jnp.float32).reshape(N_KV_HEADS, G)[None, None, :, :, None, None]
    m = jnp.maximum(jnp.max(scores, axis=-1, keepdims=True), sink)
    p = jnp.exp(scores - m)
    p = p / (jnp.sum(p, axis=-1, keepdims=True) + jnp.exp(sink - m))
    out = jnp.einsum("bckgqs,bcskd->bcqkgd", p.astype(v.dtype), vb)
    return out.reshape(B, T, Q_DIM)

def peer_ffn(xn, w_q, sub_keys, u_tab, v_tab):
    B, T, D = xn.shape
    q = (xn @ w_q).reshape(B, T, PEER_HEADS, 2, PEER_HALF).astype(jnp.float32)
    s = jnp.einsum("bthpd,hpnd->bthpn", q, sub_keys.astype(jnp.float32))
    s1, i1 = lax.top_k(s[..., 0, :], PEER_TOPK)
    s2, i2 = lax.top_k(s[..., 1, :], PEER_TOPK)
    cand_s = (s1[..., :, None] + s2[..., None, :]).reshape(B, T, PEER_HEADS, PEER_TOPK * PEER_TOPK)
    cand_i = (i1[..., :, None] * N_KEYS + i2[..., None, :]).reshape(B, T, PEER_HEADS, PEER_TOPK * PEER_TOPK)
    top_s, pos = lax.top_k(cand_s, PEER_TOPK)
    idx = jnp.take_along_axis(cand_i, pos, axis=-1)
    gates = jax.nn.softmax(top_s, axis=-1)
    nb = (B * T) // PEER_BLOCK
    hk = PEER_HEADS * PEER_TOPK
    xb = xn.reshape(nb, PEER_BLOCK, D)
    ib = idx.reshape(nb, PEER_BLOCK, hk)
    gb = gates.reshape(nb, PEER_BLOCK, hk).astype(xn.dtype)

    def block(args):
        xt, it, gt = args
        hid = jnp.einsum("tkd,td->tk", u_tab[it], xt)
        act = jax.nn.gelu(hid) * gt
        return jnp.einsum("tk,tkd->td", act, v_tab[it])

    y = lax.map(block, (xb, ib, gb))
    return y.reshape(B, T, D)

def setup_inputs(seed: int = 0) -> dict:
    key = jax.random.key(seed)
    ks = jax.random.split(key, 20)
    f32 = jnp.float32
    L = DEPTH

    def nrm(k, shape, scale):
        return jax.random.normal(k, shape, f32) * scale

    return {
        "x": jax.random.normal(ks[0], (BATCH, SEQ, D_MODEL), f32),
        "norm_mix_g": 1.0 + nrm(ks[1], (L, D_MODEL), 0.01),
        "w_in": nrm(ks[2], (L, D_MODEL, IN_DIM), D_MODEL ** -0.5),
        "conv_dw_w": nrm(ks[3], (L, CONV_WIDTH, CONV_DIM), CONV_WIDTH ** -0.5),
        "conv_dw_b": nrm(ks[4], (L, CONV_DIM), 0.01),
        "conv_ln_g": 1.0 + nrm(ks[5], (L, CONV_DIM), 0.01),
        "conv_ln_b": nrm(ks[6], (L, CONV_DIM), 0.01),
        "w_conv_out": nrm(ks[7], (L, CONV_DIM, D_MODEL), CONV_DIM ** -0.5),
        "attn_sinks": nrm(ks[8], (L, N_Q_HEADS), 0.5),
        "w_attn_out": nrm(ks[9], (L, Q_DIM, D_MODEL), Q_DIM ** -0.5),
        "w_out": nrm(ks[10], (L, D_MODEL, D_MODEL), D_MODEL ** -0.5),
        "norm_ffn_g": 1.0 + nrm(ks[11], (L, D_MODEL), 0.01),
        "peer_w_q": nrm(ks[12], (L, D_MODEL, PEER_HEADS * PEER_KEY_DIM), D_MODEL ** -0.5),
        "peer_sub_keys": nrm(ks[13], (L, PEER_HEADS, 2, N_KEYS, PEER_HALF), PEER_HALF ** -0.5),
        "peer_u": nrm(ks[14], (L, N_EXPERTS, D_MODEL), D_MODEL ** -0.5),
        "peer_v": nrm(ks[15], (L, N_EXPERTS, D_MODEL), (PEER_HEADS * PEER_TOPK) ** -0.5),
        "final_norm_g": 1.0 + nrm(ks[16], (D_MODEL,), 0.01),
    }

def reference(x, norm_mix_g, w_in, conv_dw_w, conv_dw_b, conv_ln_g, conv_ln_b, w_conv_out,
              attn_sinks, w_attn_out, w_out, norm_ffn_g, peer_w_q, peer_sub_keys, peer_u, peer_v,
              final_norm_g):
    B, T, _ = x.shape
    splits = [2 * CONV_DIM, 2 * CONV_DIM + Q_DIM, 2 * CONV_DIM + Q_DIM + KV_DIM,
              2 * CONV_DIM + Q_DIM + 2 * KV_DIM]
    h = x
    for l in range(DEPTH):
        a = rmsnorm(h, norm_mix_g[l])
        z = a @ w_in[l]
        zc, zq, zk, zv, zg = jnp.split(z, splits, axis=-1)
        y_conv = conformer_conv(zc, conv_dw_w[l], conv_dw_b[l], conv_ln_g[l], conv_ln_b[l],
                                w_conv_out[l])
        q = zq.reshape(B, T, N_Q_HEADS, HEAD_DIM)
        k = zk.reshape(B, T, N_KV_HEADS, HEAD_DIM)
        v = zv.reshape(B, T, N_KV_HEADS, HEAD_DIM)
        y_attn = banded_sink_attention(q, k, v, attn_sinks[l]) @ w_attn_out[l]
        g_conv, g_attn = jnp.split(jax.nn.sigmoid(zg), 2, axis=-1)
        h = h + (g_conv * y_conv + g_attn * y_attn) @ w_out[l]
        h = h + peer_ffn(rmsnorm(h, norm_ffn_g[l]), peer_w_q[l], peer_sub_keys[l],
                         peer_u[l], peer_v[l])
    return rmsnorm(h, final_norm_g)


_drawn_inputs = setup_inputs


def setup_inputs(seed=0):
    import zlib

    import numpy as np

    out = dict(_drawn_inputs(seed))
    spreads = {}
    factors = {'norm_mix_g': 8.0,
     'conv_dw_b': 42.258,
     'conv_ln_g': 64.0,
     'conv_ln_b': 64.0,
     'attn_sinks': 8.0,
     'norm_ffn_g': 64.0,
     'final_norm_g': 33.669}
    for name, (base, spread) in spreads.items():
        noise = np.random.default_rng([zlib.crc32(name.encode()), seed]).standard_normal(out[name].shape)
        drawn = base * np.exp(spread * noise) if base else spread * noise
        out[name] = __import__('jax').numpy.asarray(drawn.astype(out[name].dtype))
    for name, factor in factors.items():
        out[name] = (out[name] * factor).astype(out[name].dtype)
    return out
```

```python
from contextlib import ExitStack

import numpy as np

import concourse.bass as bass
from concourse import mybir

F32 = mybir.dt.float32
F32R = mybir.dt.float32r
U32 = mybir.dt.uint32
I32 = mybir.dt.int32
ALU = mybir.AluOpType
ACT = mybir.ActivationFunctionType
AX = mybir.AxisListType

P = 128
T = 512
TB = T // P
D = 2048
KD = D // P
CONV = 1024
CC = CONV // P
TAPS = 31
PAD = TAPS - 1
NQ, NKV, HD = 16, 2, 64
QDIM = NQ * HD
Q0 = 2 * CONV
K0 = Q0 + QDIM
V0 = K0 + NKV * HD
G0 = V0 + NKV * HD
CHUNK = 64
PH = 8
NK = 128
TOPK = 16
HK = PH * TOPK
RMS_EPS = 1e-6
LN_EPS = 1e-5
MASKED = -3.0e38
UK, UC = 8, 256
RING = 8
RANK_STEPS = 5 * TB + 2
HG = 4
SLOPES = [float(np.float32(np.power(np.float32(2.0), np.float32(-8.0 * (h + 1) / NQ)))) for h in range(NQ)]

U_Q = 0
U_KV = U_Q + 8
U_GLU = U_KV + 2
U_MIX = U_GLU + 16
MIX_IT = D // (2 * UC)
U_OUT = U_MIX + 2 * 6 * MIX_IT
U_PQ = U_OUT + 16
S_MIX = U_MIX
S_OUT = S_MIX + 2 * 4 * MIX_IT
S_PQ = S_OUT + 16

FREE, FULL = {}, {}


def _count_banks():
    free, full = [0] * 8, [0] * 8
    steps = [
        ("xT", [4, 4, 4, 4, 1, 0, 0, 0], [4, 4, 4, 4, 1, 0, 0, 0]),
        ("q", [2, 2, 2, 2, 0, 0, 0, 0], [0] * 8),
        ("kv", [1, 1, 0, 0, 0, 0, 0, 0], [0] * 8),
        ("kdup", [0, 0, 1, 1, 0, 0, 0, 0], [0, 0, 1, 1, 0, 0, 0, 0]),
        ("vtok", [1, 0, 0, 0, 0, 0, 0, 0], [1, 0, 0, 0, 0, 0, 0, 0]),
        ("glu", [4, 4, 4, 4, 0, 0, 0, 0], [0] * 8),
        ("attn", [0, 0, 0, 0, 16, 16, 32, 16], [0, 0, 0, 0, 16, 16, 32, 16]),
        ("mixA", [4] * 8, [0] * 8),
        ("ln", [0, 0, 0, 0, 1, 1, 0, 0], [0, 0, 0, 0, 1, 0, 0, 0]),
        ("mixB", [4] * 8, [0] * 8),
        ("out", [4] * 8, [0] * 8),
        ("xnT", [4, 4, 4, 4, 0, 0, 0, 0], [4, 4, 4, 4, 0, 0, 0, 0]),
        ("keys", [0, 0, 0, 0, 1, 1, 1, 1], [0, 0, 0, 0, 1, 1, 1, 1]),
        ("pq", [4] * 8, [0, 0, 0, 0, 4, 4, 4, 4]),
        ("end", [0] * 8, [0] * 8),
    ]
    for name, given_back, filled in steps:
        FREE[name], FULL[name] = list(free), list(full)
        free = [a + b for a, b in zip(free, given_back)]
        full = [a + b for a, b in zip(full, filled)]


_count_banks()


def build(nc, x, norm_mix_g, w_in, conv_dw_w, conv_dw_b, conv_ln_g, conv_ln_b, w_conv_out, attn_sinks,
          w_attn_out, w_out, norm_ffn_g, peer_w_q, peer_sub_keys, peer_u, peer_v, final_norm_g, out):
    ctx = ExitStack()
    with ctx:
        def sb(name, shape, dt=F32, stack=ctx):
            return stack.enter_context(nc.sbuf_tensor(name, shape, dt))

        def sem(name):
            return ctx.enter_context(nc.semaphore(name))

        ident = sb("ident", [P, P])
        lnmean = sb("lnmean", [P, P])
        negdist = sb("negdist", [P, 2 * P])
        disti = sb("disti", [P, 2 * P], I32)
        vecs = sb("vecs", [P, 40 + 8 * TAPS])
        sinks = sb("sinks", [P, NQ])
        stat = sb("stat", [P, 16])
        soft = sb("soft", [P, 2, 6, HG])
        iota16i = sb("iota16i", [P, TOPK], I32)
        iota16 = sb("iota16", [P, TOPK])
        XH = sb("XH", [P, TB, D])
        B = sb("B", [P, CC * (T + PAD) + QDIM // P * T])
        G = sb("G", [P, 6400])
        g1T, cbT, lgT, lbT = vecs[:, 0:16], vecs[:, 16:24], vecs[:, 24:32], vecs[:, 32:40]
        cwT = vecs[:, 40:40 + 8 * TAPS].rearrange("p (t c) -> p t c", c=CC)
        xhf = XH[:, :, :].rearrange("p m n -> p (m n)")
        mixT = xhf.rearrange("p (k t) -> p k t", t=T)
        qT = xhf[:, 0:4096].rearrange("p (c t) -> p c t", t=T)
        kT = xhf[:, 4096:5120].rearrange("p (g t) -> p g t", g=NKV)
        vtok = xhf[:, 5120:5632].rearrange("p (m d) -> p m d", d=P)
        Sc = xhf[:, 5632:7680].rearrange("p (b h s) -> p b h s", b=2, h=HG)
        uT = B[:, 0:CC * (T + PAD)].rearrange("p (c t) -> p c t", c=CC)
        OT = B[:, CC * (T + PAD):].rearrange("p (c t) -> p c t", t=T)
        xn = B[:, 0:TB * D].rearrange("p (m n) -> p m n", m=TB)
        PT = G[:, 0:2048].rearrange("p (b h s t) -> p b h s t", b=2, h=HG, s=2)
        qblk = G[:, 2048:3072].rearrange("p (c t) -> p c t", t=P)
        vblk = G[:, 3072:3328].rearrange("p (s d) -> p s d", s=2)
        acc = G[:, 3328:3840]
        kblk = G[:, 3840:4352].rearrange("p (g t) -> p g t", g=NKV)
        mu = G[:, 4352:4864]
        rstd = G[:, 4864:5376]
        sq = G[:, 5376:6400].rearrange("p (b t) -> p b t", b=2)
        vrows = G[:, 5376:5760].rearrange("p (r n) -> p r n", n=P)
        kvT = G[:, 4352:5376].rearrange("p (b t) -> p b t", b=2)
        sig = G[:, 0:2048].rearrange("p (b t) -> p b t", t=T)
        glusig = sq
        skT = G[:, 0:2048].rearrange("p (i n) -> p i n", n=NK)
        skraw = G[:, 2048:4096].rearrange("p (i d) -> p i d", d=P)
        g2b = G[:, 4096:6144]
        qchunk = G[:, 2048:3072].rearrange("p (b t) -> p b t", b=2)
        sc = G[:, 3072:3584].rearrange("p (m n) -> p m n", m=TB)
        topv = G[:, 4096:5120].rearrange("p (m i k) -> p m i k", m=TB, i=2 * PH)
        topi = G[:, 5120:6144].rearrange("p (m i k) -> p m i k", m=TB, i=2 * PH)
        bestv = G[:, 3584:3648].rearrange("p (m k) -> p m k", m=TB)
        besti = G[:, 3648:3712].bitcast(U32).rearrange("p (m k) -> p m k", m=TB)

        early = ExitStack()
        aTh = sb("aTh", [P, KD, T], F32R, early)
        aTl = sb("aTl", [P, KD, T], F32R, early)
        Wh = sb("Wh", [P, 2, UK, UC], F32R, early)
        Wl = sb("Wl", [P, 2, UK, UC], F32R, early)
        raw = sb("raw", [P, 2, UK, UC], F32, early)
        early.close()
        ring = sb("ring", [P, RING, D])
        gfin = sb("gfin", [P, D])
        cand = sb("cand", [P, PH, TOPK, TOPK])
        pick = sb("pick", [P, PH, TOPK, TOPK])
        tops = sb("tops", [P, PH, TOPK])
        tpos = sb("tpos", [P, PH, TOPK], U32)
        tposp = sb("tposp", [P, 2, PH, TOPK], U32)
        tposf = sb("tposf", [P, 2, PH, TOPK])
        isel = sb("isel", [P, 2, PH, TOPK])
        rs = sb("rs", [P, 2, PH])
        gates = sb("gates", [P, TB, HK])
        idx = sb("idx", [P, TB, HK], U32)
        idxs = sb("idxs", [P, 2 * RING], U32)
        hid = sb("hid", [P, HK])
        hact = sb("hact", [P, HK])

        PS = ctx.enter_context(nc.psum_tensor("PS", [P, 8, T], F32))
        xn_ps = PS[:, 0:4, :].rearrange("p b t -> p (b t)")
        y_ps = PS[:, 4:8, :].rearrange("p b t -> p (b t)")

        w_loaded = [sem("w_loaded0"), sem("w_loaded1")]
        hi_done, lo_done = sem("hi_done"), sem("lo_done")
        halves = sem("halves")
        full = [sem(f"bank_full{b}") for b in range(8)]
        free = [sem(f"bank_free{b}") for b in range(8)]
        x_loaded, consts_loaded, keys_loaded, x_reloaded, gfin_loaded = (
            sem(n) for n in ("x_loaded", "consts_loaded", "keys_loaded", "x_reloaded", "gfin_loaded"))
        pool_const, dve_const = sem("pool_const"), sem("dve_const")
        squares_done, meansq_done, std_done, norm_done = (
            sem(n) for n in ("squares_done", "meansq_done", "std_done", "norm_done"))
        aT_hi, aT_lo = sem("aT_hi"), sem("aT_lo")
        glu_done, conv_step = sem("glu_done"), sem("conv_step")
        centred, squared, sq_used, var_ready, lnstd_done, ln_step, u_ready = (
            sem(n) for n in ("centred", "squared", "sq_used", "var_ready", "lnstd_done", "ln_step", "u_ready"))
        blk_staged = sem("blk_staged")
        attn_step, negmax_ready, exp_done, p_ready = (
            sem(n) for n in ("attn_step", "negmax_ready", "exp_done", "p_ready"))
        mix_ready = sem("mix_ready")
        topk_step, route_step, sub_ready, gexp_done, idx_ready = (
            sem(n) for n in ("topk_step", "route_step", "sub_ready", "gexp_done", "idx_ready"))
        staged = sem("staged")
        gathered = [sem(f"gathered{s}") for s in range(RING)]
        tile_used = sem("tile_used")
        y_cleared = sem("y_cleared")
        xn_in_psum, gelu_done, hact_ready = sem("xn_in_psum"), sem("gelu_done"), sem("hact_ready")
        y_added, fin_sq, fin_ms, fin_std, fin_step, out_ready, stored = (
            sem(n) for n in ("y_added", "fin_sq", "fin_ms", "fin_std", "fin_step", "out_ready", "stored"))

        block = ctx.enter_context(nc.Block())

        @block.sync
        def _(sp):
            xt = x[0].rearrange("(m p) n -> p m n", p=P)
            for m in range(TB):
                sp.dma_start(XH[:, m, :], xt[:, m, :]).then_inc(x_loaded, 16)
            rows = [norm_mix_g[0].rearrange("(k p) -> k p", p=P), conv_dw_b[0].rearrange("(k p) -> k p", p=P),
                    conv_ln_g[0].rearrange("(k p) -> k p", p=P), conv_ln_b[0].rearrange("(k p) -> k p", p=P)]
            at = 0
            for r in rows:
                sp.dma_start(vrows[at:at + r.shape[0], 0, :], r).then_inc(consts_loaded, 16)
                at += r.shape[0]
            cw = conv_dw_w[0].rearrange("t (c p) -> (t c) p", p=P)
            half = 4 * TAPS
            for j in range(2):
                sp.dma_start(vrows[0:half, 1 + j, :], cw[j * half:(j + 1) * half, :]).then_inc(consts_loaded, 16)
            sp.dma_start(sinks[:, :], attn_sinks[0:1, :].to_broadcast([P, NQ])).then_inc(consts_loaded, 16)

            def load(src, k0, c0, slot):
                sp.nop(nofuse=True)
                view = src[k0 * P:(k0 + UK) * P, :].rearrange("(k p) n -> p k n", p=P)
                sp.dma_start(raw[:, slot, :, :], view[:, :, bass.ds(c0, UC)]).then_inc(w_loaded[slot], 16)

            def q_units(it):
                for u in range(4):
                    if it or u >= 2:
                        sp.wait_ge(lo_done, 4 * it + u - 1)
                    load(w_in[0], (u % 2) * UK, it * 2 * UC + Q0 + u // 2 * UC, u % 2)

            q_units(0)
            q_units(1)
            for u in range(2):
                sp.wait_ge(lo_done, U_KV + u - 1)
                load(w_in[0], u * UK, K0, u)
            with sp.Fori(0, 4) as g:
                for u in range(4):
                    sp.wait_ge(lo_done, g * 4 + (U_GLU + u - 1))
                    load(w_in[0], (u % 2) * UK, g * UC + (CONV if u < 2 else 0), u % 2)

            for branch, gate0, w_branch in ((0, G0 + D, w_attn_out), (1, G0, w_conv_out)):
                with sp.Fori(0, MIX_IT) as g:
                    n0, s0 = U_MIX + 6 * MIX_IT * branch, S_MIX + 4 * MIX_IT * branch
                    for u in range(6):
                        if u < 2:
                            sp.wait_ge(halves, g * 12 + 2 * (n0 + u - 1))
                        else:
                            sp.wait_ge(lo_done, g * 4 + (s0 + u - 1))
                        if u < 4:
                            load(w_in[0], (u % 2) * UK, g * 2 * UC + (gate0 + u // 2 * UC), u % 2)
                        else:
                            load(w_branch[0], 0, g * 2 * UC + (u % 2) * UC, u % 2)

            def out_units(it, first):
                for u in range(4):
                    if first and u < 2:
                        sp.wait_ge(halves, 2 * (U_OUT + u - 1))
                    else:
                        sp.wait_ge(lo_done, it * 4 + (S_OUT + u - 1))
                    load(w_out[0], (u % 2) * UK, it * 2 * UC + (u // 2) * UC, u % 2)

            out_units(0, True)
            with sp.Fori(1, 4) as it:
                out_units(it, False)
            sp.dma_start(skraw, peer_sub_keys[0].rearrange("h s n d -> n (h s) d")).then_inc(keys_loaded, 16)
            sp.dma_start(g2b, norm_ffn_g[0:1, :].to_broadcast([P, D])).then_inc(keys_loaded, 16)
            with sp.Fori(0, 4) as it:
                for u in range(4):
                    sp.wait_ge(lo_done, it * 4 + (S_PQ + u - 1))
                    load(peer_w_q[0], (u % 2) * UK, it * 2 * UC + (u // 2) * UC, u % 2)
            sp.wait_ge(topk_step, RANK_STEPS * 2 * PH)
            sp.dma_start(gfin[:, :], final_norm_g.rearrange("(a n) -> a n", a=1).to_broadcast([P, D])).then_inc(gfin_loaded, 16)
            ot = out[0].rearrange("(m p) n -> p m n", p=P)
            with sp.Fori(0, TB) as m:
                sp.wait_ge(out_ready, m + 1)
                sp.dma_start(ot[:, bass.ds(m, 1), :], XH[:, bass.ds(m, 1), :]).then_inc(stored, 16)
            sp.wait_ge(stored, 16 * TB)


        @block.gpsimd
        def _(pool):
            pool.memset(ident[:, :], 0.0).then_inc(pool_const, 1)
            pool.wait_ge(pool_const, 1)
            pool.affine_select(out=ident[:, :], in_=ident[:, :], compare_op=ALU.not_equal, fill=1.0,
                               base=0, pattern=[[-1, P]], channel_multiplier=1).then_inc(pool_const, 1)
            pool.iota(disti[:, :], pattern=[[-1, 2 * P]], base=P, channel_multiplier=1).then_inc(pool_const, 1)
            pool.iota(iota16i[:, :], pattern=[[1, TOPK]], base=0, channel_multiplier=0).then_inc(pool_const, 1)

            def stage(m, first):
                if first:
                    for b in range(4):
                        pool.wait_ge(free[b], FREE["glu"][b])
                    pool.tensor_copy(qblk, qT[:, :, 0:P]).then_inc(blk_staged, 1)
                    pool.tensor_copy(kblk[:, :, P:], kT[:, :, 0:P]).then_inc(blk_staged, 1)
                    pool.tensor_copy(vblk[:, 1, :], vtok[:, 0, :]).then_inc(blk_staged, 1)
                else:
                    pool.wait_ge(full[5], m * 4 + FULL["attn"][5])
                    pool.wait_ge(full[6], m * 8 + FULL["attn"][6])
                    pool.tensor_copy(qblk, qT[:, :, bass.ds(m * P, P)]).then_inc(blk_staged, 1)
                    pool.tensor_copy(kblk, kT[:, :, bass.ds((m - 1) * P, 2 * P)]).then_inc(blk_staged, 1)
                    pool.tensor_copy(vblk, vtok[:, bass.ds(m - 1, 2), :]).then_inc(blk_staged, 1)

            stage(0, True)
            with pool.Fori(1, TB) as m:
                stage(m, False)

            rounds = HK // (2 * RING)
            with pool.Fori(0, TB) as m:
                pool.wait_ge(idx_ready, m + 1)
                pool.nop(nofuse=True)
                for part, table in enumerate((peer_u, peer_v)):
                    with pool.Fori(0, rounds) as r:
                        for h in range(2):
                            pool.tensor_copy(idxs[:, h * RING:(h + 1) * RING],
                                             idx[:, bass.ds(m, 1), bass.ds(r * 2 * RING + h * RING, RING)]
                                             .rearrange("p a k -> p (a k)")).then_inc(staged, 1)
                            pool.wait_ge(staged, m * (4 * rounds) + r * 2 + (part * 2 * rounds + h + 1))
                            for s in range(RING):
                                pool.wait_ge(tile_used, m * 2 * HK + r * 2 * RING + (part * HK + h * RING + s + 1))
                                pool.nop(nofuse=True)
                                pool.indirect_dma_start(
                                    ring[:, s, :], None, table[0],
                                    bass.IndirectOffsetOnAxis(idxs[:, h * RING + s:h * RING + s + 1], 0),
                                ).then_inc(gathered[s], 16)

        @block.scalar
        def _(act):
            act.wait_ge(x_loaded, 16 * TB)
            for m in range(TB):
                act.activation(aTl[:, 4 * m:4 * m + 4, :].rearrange("p k t -> p (k t)"), XH[:, m, :], ACT.Square,
                               accum_out=stat[:, m:m + 1]).then_inc(squares_done, 1)
            act.wait_ge(meansq_done, 1)
            act.activation(stat[:, 8:12], stat[:, 4:8], ACT.Sqrt).then_inc(std_done, 1)
            act.wait_ge(full[4], 1)
            act.activation(vecs[:, :], PS[:, 4, 0:40 + 8 * TAPS], ACT.Copy).then_inc(free[4], 1)
            act.wait_ge(free[4], 1)
            for k in range(KD):
                act.wait_ge(full[k % 4], k // 4 + 1)
                act.activation(aTh[:, k, :], PS[:, k % 4, :], ACT.Copy, scale=g1T[:, k:k + 1]).then_inc(aT_hi, 1)

            def hi(n, slot, loads, first=False):
                act.wait_ge(w_loaded[slot], loads)
                if not first:
                    act.wait_ge(halves, n * 2 - 2)
                act.activation(Wh[:, slot, :, :], raw[:, slot, :, :], ACT.Copy).then_inc(hi_done, 1)

            def hi4(it, base, u):
                hi(it * 4 + (base + u), u % 2, it * 32 + 16 * ((base + u) // 2 + 1))

            hi(0, 0, 16, True)
            for it in range(2):
                for u in range(4):
                    n = it * 4 + u + 1
                    hi(n, n % 2, 16 * (n // 2 + 1), n < 2)
                    if u % 2:
                        act.wait_ge(halves, 2 * n)
                        for b in range(2):
                            act.activation(qT[:, it * 4 + u // 2 * 2 + b, :], PS[:, u // 2 * 2 + b, :], ACT.Copy,
                                           scale=HD ** -0.5).then_inc(free[u // 2 * 2 + b], 1)
            hi4(0, U_KV, 1)
            hi4(0, U_KV, 2)
            act.wait_ge(halves, 2 * U_GLU)
            for b in range(2):
                act.activation(kvT[:, b, :], PS[:, b, :], ACT.Copy).then_inc(free[b], 1)
            for b in (2, 3):
                act.wait_ge(full[b], FULL["kdup"][b] + 1)
                act.activation(kT[:, b - 2, :], PS[:, b, :], ACT.Copy).then_inc(free[b], 1)
            act.wait_ge(full[0], FULL["vtok"][0] + 1)
            act.activation(vtok, PS[:, 0, :].rearrange("p (m d) -> p m d", m=TB), ACT.Copy).then_inc(free[0], 1)

            def glu_attn(g, first):
                lo = P if first else 0

                def exps(hg):
                    b = hg % 2
                    act.wait_ge(negmax_ready, g * 4 + (hg + 1))
                    for i in range(HG):
                        act.activation(Sc[:, b, i, lo:], Sc[:, b, i, lo:], ACT.Exp, bias=soft[:, b, 1, i:i + 1],
                                       accum_out=soft[:, b, 2, i:i + 1])
                    act.activation(soft[:, b, 4, :], soft[:, b, 3, :], ACT.Exp).then_inc(exp_done, 1)

                def pt_copy(hg):
                    if not (first and hg < 2):
                        act.wait_ge(full[6], g * 8 + (FULL["attn"][6] + 2 * hg - 2))
                    for j in range(2):
                        act.wait_ge(full[6 + j], g * (8 - 4 * j) + (FULL["attn"][6 + j] + (2 - j) * hg + 1))
                        act.activation(PT[:, hg % 2, 2 * j:2 * j + 2, lo // P:, :],
                                       PS[:, 6 + j, :].rearrange("p (h s t) -> p h s t", h=2, s=2)[:, :, lo // P:, :],
                                       ACT.Copy).then_inc(free[6 + j], 1)

                def o_copy(hg):
                    act.wait_ge(full[6], g * 8 + (FULL["attn"][6] + 2 * hg + 2))
                    act.activation(OT[:, 2 * hg:2 * hg + 2, bass.ds(g * P, P)],
                                   PS[:, 6, 0:2 * P].rearrange("p (c t) -> p c t", c=2), ACT.Copy).then_inc(free[6], 1)

                hi4(g, U_GLU, 1)
                hi4(g, U_GLU, 2)
                exps(0)
                exps(1)
                hi4(g, U_GLU, 3)
                pt_copy(0)
                o_copy(0)
                if not first:
                    act.wait_ge(glu_done, g * 2)
                for b in range(2):
                    act.activation(glusig[:, b, :], PS[:, b, :], ACT.Sigmoid).then_inc(free[b], 1)
                exps(2)
                hi4(g, U_GLU, 4)
                pt_copy(1)
                o_copy(1)
                exps(3)
                pt_copy(2)
                o_copy(2)
                pt_copy(3)
                o_copy(3)

            glu_attn(0, True)
            with act.Fori(1, 4) as g:
                glu_attn(g, False)

            def mix(branch, g, ln):
                n0 = U_MIX + 6 * MIX_IT * branch

                def mix_hi(u):
                    hi(g * 6 + (n0 + u), u % 2, g * 48 + 16 * ((n0 + u) // 2 + 1))

                def sigmoids(first_bank, u):
                    act.wait_ge(halves, g * 12 + 2 * (n0 + u + 1))
                    for b in (first_bank, first_bank + 1):
                        act.activation(sig[:, b, :], PS[:, b, :], ACT.Sigmoid).then_inc(free[b], 1)

                mix_hi(1)
                if ln:
                    for c in range(CC):
                        act.wait_ge(centred, c + 1)
                        if c >= 2:
                            act.wait_ge(sq_used, c - 1)
                        act.activation(sq[:, c % 2, :], uT[:, c, 0:T], ACT.Square).then_inc(squared, 1)
                mix_hi(2)
                act.wait_ge(mix_ready, g * 4 + (4 * MIX_IT * branch + 1))
                sigmoids(0, 1)
                mix_hi(3)
                if ln:
                    act.wait_ge(free[5], FREE["ln"][5] + 1)
                    act.activation(rstd, rstd, ACT.Sqrt).then_inc(lnstd_done, 1)
                    for c in range(CC):
                        act.wait_ge(ln_step, 2 + c)
                        act.activation(uT[:, c, 0:T], uT[:, c, 0:T], ACT.Silu, bias=lbT[:, c:c + 1],
                                       scale=lgT[:, c:c + 1]).then_inc(u_ready, 1)
                sigmoids(2, 3)
                mix_hi(6)

            with act.Fori(0, MIX_IT) as g:
                mix(0, g, False)
            act.wait_ge(full[4], FULL["ln"][4] + 1)
            act.activation(mu, PS[:, 4, :], ACT.Copy).then_inc(free[4], 1)
            mix(1, 0, True)
            with act.Fori(1, MIX_IT) as g:
                mix(1, g, False)

            act.wait_ge(mix_ready, 8 * MIX_IT + 1)
            for k in range(4):
                act.activation(aTh[:, 4 * k:4 * k + 4, :], mixT[:, 4 * k:4 * k + 4, :], ACT.Copy).then_inc(aT_hi, 1)
            act.wait_ge(aT_lo, 4)
            act.dma_start(XH[:, :, :], x[0].rearrange("(m p) n -> p m n", p=P)).then_inc(x_reloaded, 16)
            with act.Fori(0, 4) as it:
                for u in range(4):
                    hi4(it, U_OUT, u + 1)

            for b in range(8):
                act.wait_ge(free[b], FREE["xnT"][b])
            for m in range(TB):
                act.activation(aTl[:, 4 * m:4 * m + 4, :].rearrange("p k t -> p (k t)"), XH[:, m, :], ACT.Square,
                               accum_out=stat[:, m:m + 1]).then_inc(squares_done, 1)
            act.wait_ge(meansq_done, 2)
            act.activation(stat[:, 8:12], stat[:, 4:8], ACT.Sqrt).then_inc(std_done, 1)
            for b in range(4, 8):
                act.wait_ge(full[b], FULL["keys"][b] + 1)
                act.activation(skT[:, 4 * b - 16:4 * b - 12, :], PS[:, b, :].rearrange("p (i n) -> p i n", i=4),
                               ACT.Copy).then_inc(free[b], 1)
            for k in range(KD):
                act.wait_ge(full[k % 4], FULL["xnT"][k % 4] + k // 4 + 1)
                act.activation(aTh[:, k, :], PS[:, k % 4, :], ACT.Copy).then_inc(aT_hi, 1)

            def peer_q(it, last):
                for u in range(4):
                    if not (last and u == 3):
                        hi4(it, U_PQ, u + 1)
                    if u % 2:
                        act.wait_ge(halves, it * 8 + 2 * (U_PQ + u + 1))
                        for b in range(2):
                            last_bank = 6 + b if u == 1 else 4 + b
                            act.wait_ge(full[last_bank], it + (FULL["pq"][last_bank] + u // 2))
                            act.activation(qchunk[:, b, :], PS[:, u // 2 * 2 + b, :], ACT.Copy)\
                               .then_inc(free[u // 2 * 2 + b], 1)

            with act.Fori(0, 3) as it:
                peer_q(it, False)
            peer_q(3, True)

            def gate_exp(m):
                act.wait_ge(sub_ready, m + 1)
                act.activation(tops[:, :, :], tops[:, :, :], ACT.Exp).then_inc(gexp_done, 1)

            def xn_to_psum(m):
                act.wait_ge(y_cleared, m + 1)
                act.activation(xn_ps, xn[:, bass.ds(m, 1), :].rearrange("p a n -> p (a n)"), ACT.Copy)\
                   .then_inc(xn_in_psum, 1)

            def experts(m, last):
                act.wait_ge(y_cleared, m + 2)
                act.activation(hact[:, :], hid[:, :], ACT.Gelu_apprx_tanh).then_inc(gelu_done, 1)
                if not last:
                    xn_to_psum(m + 1)
                    gate_exp(m + 1)
                act.wait_ge(y_added, m + 1)
                act.activation(pick[:, :, :, :].rearrange("p a b c -> p (a b c)"),
                               XH[:, bass.ds(m, 1), :].rearrange("p a n -> p (a n)"), ACT.Square,
                               accum_out=stat[:, 0:1]).then_inc(fin_sq, 1)
                act.wait_ge(fin_ms, m + 1)
                act.activation(stat[:, 2:3], stat[:, 1:2], ACT.Sqrt).then_inc(fin_std, 1)

            xn_to_psum(0)
            gate_exp(0)
            with act.Fori(0, TB - 1) as m:
                experts(m, False)
            experts(TB - 1, True)

        @block.tensor
        def _(pe):
            pe.wait_ge(pool_const, 4)
            pe.wait_ge(consts_loaded, 16 * 7)
            half = 4 * TAPS
            pe.transpose(PS[:, 4, 0:40], vrows[0:40, 0, :], ident[0:40, 0:40])
            for j in range(2):
                ins = pe.transpose(PS[:, 4, 40 + j * half:40 + (j + 1) * half], vrows[0:half, 1 + j, :], ident[0:half, 0:half])
            ins.then_inc(full[4], 1)

            def to_xT(src, phase):
                for k in range(KD):
                    if FREE[phase][k % 4] + k // 4:
                        pe.wait_ge(free[k % 4], FREE[phase][k % 4] + k // 4)
                    for m in range(TB):
                        ins = pe.transpose(PS[:, k % 4, m * P:(m + 1) * P], src[:, m, k * P:(k + 1) * P], ident[:, :])
                    ins.then_inc(full[k % 4], 1)

            pe.wait_ge(norm_done, TB)
            to_xT(XH, "xT")

            def unit(split, slot, bank, start, stop, k0):
                pe.wait_ge(lo_done, split)
                for b in range(2):
                    for k in range(UK):
                        for j, (w, a) in enumerate(((Wh, aTh), (Wl, aTh), (Wh, aTl))):
                            ins = pe.matmul(PS[:, bank + b, :], w[:, slot, k, b * P:(b + 1) * P], a[:, k0 + k, :],
                                            start=start and k == 0 and j == 0, stop=stop and k == UK - 1 and j == 2)
                    ins.then_inc(halves, 1)

            def group(split, bank, it, phase):
                for b in range(2):
                    pe.wait_ge(free[bank + b], it + FREE[phase][bank + b])
                unit(split, 0, bank, True, False, 0)
                unit(split + 1, 1, bank, False, True, UK)

            for it in range(2):
                group(it * 4 + 1, 0, it, "q")
                group(it * 4 + 3, 2, it, "q")
            group(U_KV + 1, 0, 0, "kv")
            pe.wait_ge(free[0], FREE["kv"][0] + 1)
            for g in range(NKV):
                pe.wait_ge(free[2 + g], FREE["kdup"][2 + g])
                for b in range(2):
                    ins = pe.matmul(PS[b * HD:(b + 1) * HD, 2 + g, :], ident[:, g * HD:(g + 1) * HD], kvT[:, 0, :],
                                    start=True, stop=True)
                ins.then_inc(full[2 + g], 1)
            pe.wait_ge(free[1], FREE["kv"][1] + 1)
            for m in range(TB):
                ins = pe.transpose(PS[:, 0, m * P:(m + 1) * P], kvT[:, 1, m * P:(m + 1) * P], ident[:, :])
            ins.then_inc(full[0], 1)

            def glu_attn(g, first):
                parts = (1,) if first else (0, 1)

                def qk(hg):
                    for i in range(HG):
                        h, bank = HG * hg + i, 4 + i % 2
                        o = (h % 2) * HD
                        if i < 2:
                            pe.wait_ge(free[bank], g * 4 + (FREE["attn"][bank] + hg)) if FREE["attn"][bank] + hg or not first else None
                        at, lo = (i // 2) * 2 * P, P if first else 0
                        ins = pe.matmul(PS[:, bank, at + lo:at + 2 * P], qblk[o:o + HD, h // 2, :],
                                        kblk[o:o + HD, h // PH, lo:], start=True, stop=True)
                        if i >= 2:
                            ins.then_inc(full[bank], 1)

                def transposes(hg):
                    pe.wait_ge(p_ready, g * 4 + (hg + 1))
                    for i in range(HG):
                        bank = 6 + i // 2
                        if i % 2 == 0 and not (first and hg == 0):
                            pe.wait_ge(free[bank], g * (8 if bank == 6 else 4) + (FREE["attn"][bank] + (2 if bank == 6 else 1) * hg))
                        for s in parts:
                            at = (i % 2) * 2 * P + s * P
                            ins = pe.transpose(PS[:, bank, at:at + P], Sc[:, hg % 2, i, s * P:(s + 1) * P], ident[:, :])
                        if i % 2:
                            ins.then_inc(full[bank], 1)

                def pv(hg):
                    pe.wait_ge(free[6], g * 8 + (FREE["attn"][6] + 2 * hg + 1))
                    pe.wait_ge(free[7], g * 4 + (FREE["attn"][7] + hg + 1))
                    for i in range(HG):
                        h = HG * hg + i
                        o = (h % 2) * HD
                        for s in parts:
                            ins = pe.matmul(PS[o:o + HD, 6, i // 2 * P:(i // 2 + 1) * P],
                                            vblk[:, s, h // PH * HD:(h // PH + 1) * HD], PT[:, hg % 2, i, s, :],
                                            start=s == parts[0], stop=s == 1)
                    ins.then_inc(full[6], 1)

                for b in range(2):
                    pe.wait_ge(free[b], g + FREE["glu"][b])
                unit(g * 4 + (U_GLU + 1), 0, 0, True, False, 0)
                pe.wait_ge(blk_staged, g * 3 + 3)
                qk(0)
                qk(1)
                unit(g * 4 + (U_GLU + 2), 1, 0, False, True, UK)
                transposes(0)
                qk(2)
                pv(0)
                for b in (2, 3):
                    pe.wait_ge(free[b], g + FREE["glu"][b])
                unit(g * 4 + (U_GLU + 3), 0, 2, True, False, 0)
                transposes(1)
                qk(3)
                pv(1)
                unit(g * 4 + (U_GLU + 4), 1, 2, False, True, UK)
                for hg in (2, 3):
                    transposes(hg)
                    pv(hg)

            glu_attn(0, True)
            with pe.Fori(1, 4) as g:
                glu_attn(g, False)

            def mix(branch, g, phase, ln):
                s0 = S_MIX + 4 * MIX_IT * branch
                group(g * 4 + (s0 + 1), 0, g, phase)
                if ln:
                    for c in range(CC):
                        pe.wait_ge(squared, c + 1)
                        pe.matmul(PS[:, 5, :], lnmean[:, :], sq[:, c % 2, :], start=c == 0, stop=c == CC - 1)\
                          .then_inc(sq_used, 1)
                group(g * 4 + (s0 + 3), 2, g, phase)
                if ln:
                    pe.wait_ge(u_ready, CC)
                for slot in range(2):
                    pe.wait_ge(w_loaded[slot], g * 48 + 16 * ((U_MIX + 6 * MIX_IT * branch) // 2 + 3))
                    for b in range(2):
                        bank = 4 + 2 * slot + b
                        pe.wait_ge(free[bank], g + FREE[phase][bank])
                        for k in range(UK):
                            ins = pe.matmul(PS[:, bank, :], raw[:, slot, k, b * P:(b + 1) * P],
                                            uT[:, k, 0:T] if branch else OT[:, k, :], start=k == 0, stop=k == UK - 1)
                        ins.then_inc(halves, 1)

            pe.wait_ge(free[6], FREE["mixA"][6])
            with pe.Fori(0, MIX_IT) as g:
                mix(0, g, "mixA", False)
            pe.wait_ge(conv_step, 1 + CC * TAPS)
            pe.wait_ge(free[4], FREE["ln"][4])
            pe.wait_ge(free[5], FREE["ln"][5])
            for c in range(CC):
                ins = pe.matmul(PS[:, 4, :], lnmean[:, :], uT[:, c, 0:T], start=c == 0, stop=c == CC - 1)
            ins.then_inc(full[4], 1)
            mix(1, 0, "mixB", True)
            with pe.Fori(1, MIX_IT) as g:
                mix(1, g, "mixB", False)

            with pe.Fori(0, 4) as it:
                for u in range(4):
                    pe.wait_ge(lo_done, it * 4 + (S_OUT + u + 1))
                    pe.wait_ge(aT_lo, 2 + 2 * (u % 2))
                    for m in range(TB):
                        bank = 4 * (u // 2) + m
                        if u % 2 == 0:
                            pe.wait_ge(free[bank], it + FREE["out"][bank])
                        for k in range(UK):
                            for j, (a, w) in enumerate(((aTh, Wh), (aTl, Wh), (aTh, Wl))):
                                ins = pe.matmul(PS[:, bank, 0:UC], a[:, (u % 2) * UK + k, m * P:(m + 1) * P],
                                                w[:, u % 2, k, :], start=u % 2 == 0 and k == 0 and j == 0,
                                                stop=u % 2 == 1 and k == UK - 1 and j == 2)
                        if m % 2:
                            ins.then_inc(halves, 1)

            pe.wait_ge(keys_loaded, 32)
            for b in range(4, 8):
                pe.wait_ge(free[b], FREE["keys"][b])
                for i in range(4):
                    ins = pe.transpose(PS[:, b, i * P:(i + 1) * P], skraw[:, 4 * (b - 4) + i, :], ident[:, :])
                ins.then_inc(full[b], 1)
            pe.wait_ge(norm_done, 2 * TB)
            to_xT(xn, "xnT")

            def scores(it, gg):
                for b in range(2):
                    bank = 4 + 2 * gg + b
                    pe.wait_ge(free[bank], it + FREE["pq"][bank])
                    pe.wait_ge(free[2 * gg + b], it + (FREE["pq"][2 * gg + b] + 1))
                    for m in range(TB):
                        ins = pe.matmul(PS[:, bank, m * P:(m + 1) * P], qchunk[:, b, m * P:(m + 1) * P],
                                        skT[:, bass.ds(it * 4 + (2 * gg + b), 1), :].rearrange("p a n -> p (a n)"),
                                        start=True, stop=True)
                    ins.then_inc(full[bank], 1)

            with pe.Fori(0, 4) as it:
                group(it * 4 + (S_PQ + 1), 0, it, "pq")
                for b in (2, 3):
                    pe.wait_ge(free[b], it + FREE["pq"][b])
                unit(it * 4 + (S_PQ + 3), 0, 2, True, False, 0)
                scores(it, 0)
                unit(it * 4 + (S_PQ + 4), 1, 2, False, True, UK)
                scores(it, 1)

        @block.vector
        def _(v):
            class Steps:

                def __init__(self, s, base=0):
                    self.s, self.base, self.n = s, base, 0

                def did(self, ins):
                    ins.then_inc(self.s, 1)
                    self.n += 1

                def wait(self):
                    v.wait_ge(self.s, self.base + self.n)
                    v.nop(nofuse=True)

            consts = Steps(dve_const)
            consts.did(v.memset(lnmean[:, :], 1.0 / CONV))
            v.wait_ge(pool_const, 4)
            consts.did(v.tensor_copy(iota16[:, :], iota16i[:, :]))
            consts.did(v.tensor_copy(negdist[:, :], disti[:, :]))
            consts.wait()
            consts.did(v.scalar_tensor_tensor(out=negdist[:, :], in0=negdist[:, :], scalar=-1.0, in1=negdist[:, :],
                                              op0=ALU.mult, op1=ALU.min))
            consts.wait()
            consts.did(v.memset(negdist[0:CHUNK, 0:CHUNK], MASKED))
            consts.did(v.memset(negdist[0:CHUNK, 3 * CHUNK:], MASKED))
            consts.did(v.memset(negdist[CHUNK:, 0:2 * CHUNK], MASKED))
            v.sem_inc(mix_ready, 1)

            def mean_square(squares, out_):
                return v.tensor_scalar(out_, squares, 1.0 / D, RMS_EPS, ALU.mult, ALU.add)

            v.wait_ge(squares_done, TB)
            mean_square(stat[:, 0:4], stat[:, 4:8]).then_inc(meansq_done, 1)
            v.wait_ge(std_done, 1)
            consts.did(v.reciprocal(stat[:, 12:16], stat[:, 8:12]))
            consts.wait()
            for m in range(TB):
                v.tensor_scalar(XH[:, m, :], XH[:, m, :], stat[:, 12 + m:13 + m], None, ALU.mult).then_inc(norm_done, 1)
            v.wait_ge(free[4], 1)
            for k in range(KD):
                v.wait_ge(aT_hi, k + 1)
                v.scalar_tensor_tensor(out=aTl[:, k, :], in0=PS[:, k % 4, :], scalar=g1T[:, k:k + 1],
                                       in1=aTh[:, k, :].bitcast(F32), op0=ALU.mult, op1=ALU.subtract)\
                 .then_inc(free[k % 4], 1)

            def lo(split, slot):
                v.wait_ge(hi_done, split)
                v.tensor_tensor(Wl[:, slot, :, :], raw[:, slot, :, :], Wh[:, slot, :, :].bitcast(F32), ALU.subtract)\
                 .then_inc(lo_done, 1)

            def conv(c, a, b):
                def one(ap):
                    return ap.rearrange("p a t -> p (a t)")
                for k in range(a, b):
                    tap = TAPS - 1 - k
                    src = one(uT[:, bass.ds(c, 1), tap:tap + T])
                    w = cwT[:, tap, bass.ds(c, 1)]
                    if k == 0:
                        v.wait_ge(glu_done, c + 1)
                    v.wait_ge(conv_step, c * TAPS + (k + 1))
                    if k == 0:
                        v.tensor_scalar(acc, src, w, cbT[:, bass.ds(c, 1)], ALU.mult, ALU.add).then_inc(conv_step, 1)
                    else:
                        v.scalar_tensor_tensor(out=one(uT[:, bass.ds(c, 1), 0:T]) if k == TAPS - 1 else acc, in0=src,
                                               scalar=w, in1=acc, op0=ALU.mult, op1=ALU.add).then_inc(conv_step, 1)

            v.memset(uT[:, :, 0:PAD], 0.0).then_inc(conv_step, 1)
            lo(1, 0)
            for n in range(U_GLU):
                lo(n + 2, (n + 1) % 2)
            v.wait_ge(consts_loaded, 16 * 7)

            def glu_attn(g, first, base):
                lo_ = P if first else 0
                steps = Steps(attn_step, base)

                def score(hg):
                    b = hg % 2
                    s_max, s_neg, _, s_sub, _, _ = (soft[:, b, j, :] for j in range(6))
                    if not (first and hg < 2):
                        v.wait_ge(full[7], g * 4 + (FULL["attn"][7] + hg - 1))
                    for i in range(HG):
                        bank, at = 4 + i % 2, (i // 2) * 2 * P
                        if i < 2:
                            v.wait_ge(full[bank], g * 4 + (FULL["attn"][bank] + hg + 1))
                        ins = v.scalar_tensor_tensor(out=Sc[:, b, i, lo_:], in0=negdist[:, lo_:],
                                                     scalar=SLOPES[HG * hg + i], in1=PS[:, bank, at + lo_:at + 2 * P],
                                                     op0=ALU.mult, op1=ALU.add)
                        if i >= 2:
                            ins.then_inc(free[bank], 1)
                        else:
                            steps.did(ins)
                    for bank in (4, 5):
                        v.wait_ge(free[bank], g * 4 + (FREE["attn"][bank] + hg + 1))
                    steps.wait()
                    steps.did(v.tensor_reduce(s_max, Sc[:, b, :, lo_:], AX.X, ALU.max))
                    steps.wait()
                    steps.did(v.tensor_tensor(s_max, s_max, sinks[:, HG * hg:HG * (hg + 1)], ALU.max))
                    steps.wait()
                    steps.did(v.tensor_scalar(s_neg, s_max, -1.0, None, ALU.mult))
                    v.tensor_tensor(s_sub, sinks[:, HG * hg:HG * (hg + 1)], s_max, ALU.subtract)\
                     .then_inc(negmax_ready, 1)

                def norm(hg):
                    b = hg % 2
                    s_sum, s_exp, s_inv = soft[:, b, 2, :], soft[:, b, 4, :], soft[:, b, 5, :]
                    v.wait_ge(exp_done, g * 4 + (hg + 1))
                    steps.did(v.tensor_tensor(s_inv, s_sum, s_exp, ALU.add))
                    steps.wait()
                    steps.did(v.reciprocal(s_inv, s_inv))
                    steps.wait()
                    v.tensor_tensor(Sc[:, b, :, lo_:], Sc[:, b, :, lo_:],
                                    s_inv.unsqueeze(2).to_broadcast([P, HG, 2 * P - lo_]), ALU.mult).then_inc(p_ready, 1)

                def glu_lo(u):
                    lo(g * 4 + (U_GLU + u + 1), u % 2)

                glu_lo(1)
                score(0)
                score(1)
                glu_lo(2)
                norm(0)
                norm(1)
                score(2)
                glu_lo(3)
                norm(2)
                score(3)
                glu_lo(4)
                norm(3)
                v.wait_ge(halves, g * 8 + 2 * (U_GLU + 4))
                for b in range(2):
                    v.wait_ge(free[b], g + (FREE["glu"][b] + 1))
                    v.tensor_tensor(uT[:, bass.ds(g * 2 + b, 1), PAD:].rearrange("p a t -> p (a t)"),
                                    PS[:, 2 + b, :], glusig[:, b, :], ALU.mult).then_inc(free[2 + b], 1)
                for b in range(2):
                    v.wait_ge(free[2 + b], g + (FREE["glu"][2 + b] + 1))
                    v.sem_inc(glu_done, 1)
                return steps.n

            per_block = glu_attn(0, True, 0)
            with v.Fori(1, TB) as g:
                glu_attn(g, False, g * per_block)

            def mix(branch, g, phase, ln):
                n0, s0 = U_MIX + 6 * MIX_IT * branch, S_MIX + 4 * MIX_IT * branch
                for u in (1, 2, 3):
                    lo(g * 4 + (s0 + u + 1), u % 2)
                    if branch == 0:
                        conv(g * 2 + (0 if u < 3 else 1), *((0, 16), (16, TAPS), (0, 16))[u - 1])
                    if ln and u == 2:
                        v.wait_ge(sq_used, CC)
                        v.tensor_scalar(rstd, PS[:, 5, :], LN_EPS, None, ALU.add).then_inc(free[5], 1)
                    if ln and u == 3:
                        v.wait_ge(lnstd_done, 1)
                        steps = Steps(ln_step)
                        steps.did(v.reciprocal(rstd, rstd))
                        steps.wait()
                        for c in range(CC):
                            steps.did(v.tensor_tensor(uT[:, c, 0:T], uT[:, c, 0:T], rstd, ALU.mult))
                for j in range(4):
                    bank = 4 + j
                    chunk = mixT[:, bass.ds(g * 4 + j, 1), :].rearrange("p a t -> p (a t)")
                    if j % 2 == 0:
                        v.wait_ge(halves, g * 12 + 2 * (n0 + 5 + j // 2))
                    v.wait_ge(free[j], g + (FREE[phase][j] + 1))
                    v.tensor_tensor(sig[:, j, :], PS[:, bank, :], sig[:, j, :], ALU.mult).then_inc(free[bank], 1)
                    if j % 2:
                        for b in (j - 1, j):
                            v.wait_ge(free[4 + b], g + (FREE[phase][4 + b] + 1))
                            chunk = mixT[:, bass.ds(g * 4 + b, 1), :].rearrange("p a t -> p (a t)")
                            if branch == 0:
                                v.tensor_copy(chunk, sig[:, b, :]).then_inc(mix_ready, 1)
                            else:
                                v.tensor_tensor(chunk, chunk, sig[:, b, :], ALU.add).then_inc(mix_ready, 1)
                    if j == 1:
                        lo(g * 4 + (s0 + 5), 0)
                if branch == 0:
                    conv(g * 2 + 1, 16, TAPS)

            with v.Fori(0, MIX_IT) as g:
                mix(0, g, "mixA", False)
            v.wait_ge(free[4], FREE["ln"][4] + 1)
            for c in range(CC):
                v.tensor_tensor(uT[:, c, 0:T], uT[:, c, 0:T], mu, ALU.subtract).then_inc(centred, 1)
            mix(1, 0, "mixB", True)
            with v.Fori(1, MIX_IT) as g:
                mix(1, g, "mixB", False)
            for k in range(4):
                v.wait_ge(aT_hi, KD + k + 1)
                v.tensor_tensor(aTl[:, 4 * k:4 * k + 4, :], mixT[:, 4 * k:4 * k + 4, :],
                                aTh[:, 4 * k:4 * k + 4, :].bitcast(F32), ALU.subtract).then_inc(aT_lo, 1)

            with v.Fori(0, 4) as it:
                for u in range(4):
                    lo(it * 4 + (S_OUT + u + 2), (u + 1) % 2)
                    if u % 2:
                        v.wait_ge(x_reloaded, 16)
                        v.wait_ge(halves, it * 8 + 2 * (U_OUT + u + 1))
                        for m in range(TB):
                            bank = 4 * (u // 2) + m
                            h = XH[:, m, bass.ds(it * 2 * UC + (u // 2) * UC, UC)]
                            v.tensor_tensor(h, PS[:, bank, 0:UC], h, ALU.add).then_inc(free[bank], 1)

            v.wait_ge(squares_done, 2 * TB)
            mean_square(stat[:, 0:4], stat[:, 4:8]).then_inc(meansq_done, 1)
            v.wait_ge(std_done, 2)
            consts.did(v.reciprocal(stat[:, 12:16], stat[:, 8:12]))
            consts.wait()
            v.wait_ge(keys_loaded, 32)
            for m in range(TB):
                v.scalar_tensor_tensor(out=xn[:, m, :], in0=XH[:, m, :], scalar=stat[:, 12 + m:13 + m], in1=g2b,
                                       op0=ALU.mult, op1=ALU.mult).then_inc(norm_done, 1)
            for k in range(KD):
                v.wait_ge(aT_hi, KD + 4 + k + 1)
                v.tensor_tensor(aTl[:, k, :], PS[:, k % 4, :], aTh[:, k, :].bitcast(F32), ALU.subtract)\
                 .then_inc(free[k % 4], 1)

            def rank(it, j):
                bank = 4 + j
                i = it * 4 + j
                steps = Steps(topk_step, it * (4 * RANK_STEPS) + RANK_STEPS * j)
                v.wait_ge(full[bank], it + (FULL["pq"][bank] + 1))
                v.nop(nofuse=True)

                def src(m):
                    return PS[:, bank, m * NK:(m + 1) * NK]

                for m in range(TB):
                    steps.did(v.max(bestv[:, m, 0:8], src(m)))
                steps.wait()
                for m in range(TB):
                    steps.did(v.max_index(besti[:, m, 0:8], bestv[:, m, 0:8], src(m)))
                for m in range(TB):
                    steps.did(v.match_replace(sc[:, m, :], bestv[:, m, 0:8], src(m), MASKED))
                steps.wait()
                v.sem_inc(free[bank], 1)
                for m in range(TB):
                    steps.did(v.max(bestv[:, m, 8:16], sc[:, m, :]))
                steps.wait()
                for m in range(TB):
                    steps.did(v.max_index(besti[:, m, 8:16], bestv[:, m, 8:16], sc[:, m, :]))
                steps.wait()
                steps.did(v.tensor_copy(topv[:, :, bass.ds(i, 1), :].rearrange("p m a k -> p m (a k)"), bestv))
                steps.did(v.tensor_copy(topi[:, :, bass.ds(i, 1), :].rearrange("p m a k -> p m (a k)"), besti))
                steps.wait()

            def peer_q(it, last):
                for u in range(4):
                    if not (last and u == 3):
                        lo(it * 4 + (S_PQ + u + 2), (u + 1) % 2)
                    if u == 2:
                        rank(it, 0)
                        rank(it, 1)
                    if u == 3:
                        rank(it, 2)
                        rank(it, 3)

            with v.Fori(0, 3) as it:
                peer_q(it, False)
            peer_q(3, True)

            def route(m, base):
                steps = Steps(route_step, base)
                one = bass.ds(m, 1)
                tv = topv[:, one, :, :].rearrange("p a (h s) k -> p (a h) s k", s=2)
                steps.did(v.tensor_tensor(cand[:, :, :, :],
                                          tv[:, :, 0, :].unsqueeze(3).to_broadcast([P, PH, TOPK, TOPK]),
                                          tv[:, :, 1, :].unsqueeze(2).to_broadcast([P, PH, TOPK, TOPK]), ALU.add))
                steps.wait()
                cf = cand[:, :, :, :].rearrange("p h a b -> p h (a b)")
                for a in (0, 8):
                    for h in range(PH):
                        steps.did(v.max(tops[:, h, a:a + 8], cf[:, h, :]))
                    steps.wait()
                    for h in range(PH):
                        steps.did(v.max_index(tpos[:, h, a:a + 8], tops[:, h, a:a + 8], cf[:, h, :]))
                    steps.wait()
                    if a == 0:
                        for h in range(PH):
                            steps.did(v.match_replace(cf[:, h, :], tops[:, h, 0:8], cf[:, h, :], MASKED))
                        steps.wait()
                steps.did(v.tensor_scalar(tposp[:, 0, :, :], tpos[:, :, :], 4, None, ALU.logical_shift_right))
                steps.did(v.tensor_scalar(tposp[:, 1, :, :], tpos[:, :, :], TOPK - 1, None, ALU.bitwise_and))
                steps.did(v.tensor_copy(rs[:, 0, :], tops[:, :, 0]))
                steps.wait()
                steps.did(v.tensor_copy(tposf[:, :, :, :], tposp[:, :, :, :]))
                v.tensor_tensor(tops[:, :, :], tops[:, :, :], rs[:, 0, :].unsqueeze(2).to_broadcast([P, PH, TOPK]),
                                ALU.subtract).then_inc(sub_ready, 1)
                steps.wait()
                tif = topi[:, one, :, :].rearrange("p a (h s) k -> p (a h) s k", s=2)
                for s in range(2):
                    steps.did(v.tensor_tensor(pick[:, :, :, :].rearrange("p h a b -> p (h a) b"),
                                              tposf[:, s, :, :].rearrange("p h k -> p (h k)").unsqueeze(2).to_broadcast([P, HK, TOPK]),
                                              iota16[:, :].unsqueeze(1).to_broadcast([P, HK, TOPK]), ALU.is_equal))
                    steps.wait()
                    steps.did(v.tensor_tensor(pick[:, :, :, :], pick[:, :, :, :],
                                              tif[:, :, s, :].unsqueeze(2).to_broadcast([P, PH, TOPK, TOPK]), ALU.mult))
                    steps.wait()
                    steps.did(v.tensor_reduce(isel[:, s, :, :], pick[:, :, :, :], AX.X, ALU.add))
                    steps.wait()
                v.scalar_tensor_tensor(out=idx[:, one, :].rearrange("p a k -> p (a k)"),
                                       in0=isel[:, 0, :, :].rearrange("p h k -> p (h k)"), scalar=float(NK),
                                       in1=isel[:, 1, :, :].rearrange("p h k -> p (h k)"), op0=ALU.mult, op1=ALU.add)\
                 .then_inc(idx_ready, 1)
                v.wait_ge(gexp_done, m + 1)
                steps.did(v.tensor_reduce(rs[:, 0, :], tops[:, :, :], AX.X, ALU.add))
                steps.wait()
                steps.did(v.reciprocal(rs[:, 1, :], rs[:, 0, :]))
                steps.wait()
                steps.did(v.tensor_tensor(gates[:, one, :].rearrange("p a (h k) -> p (a h) k", h=PH), tops[:, :, :],
                                          rs[:, 1, :].unsqueeze(2).to_broadcast([P, PH, TOPK]), ALU.mult))
                steps.wait()
                return steps.n

            def experts(m, last, per_route):
                v.wait_ge(xn_in_psum, m + 1)
                v.nop(nofuse=True)
                with v.Fori(0, HK // RING) as r:
                    for s in range(RING):
                        v.wait_ge(gathered[s], m * (32 * (HK // RING)) + r * 16 + 16)
                        v.scalar_tensor_tensor(out=ring[:, s, :], in0=ring[:, s, :], scalar=1.0, in1=xn_ps,
                                               op0=ALU.mult, op1=ALU.mult,
                                               accum_out=hid[:, bass.ds(r * RING + s, 1)]).then_inc(tile_used, 1)
                v.wait_ge(tile_used, m * 2 * HK + (RING + HK))
                v.memset(y_ps, 0.0).then_inc(y_cleared, 1)
                v.wait_ge(gelu_done, m + 1)
                v.tensor_tensor(hact[:, :], hact[:, :], gates[:, bass.ds(m, 1), :].rearrange("p a k -> p (a k)"), ALU.mult)\
                 .then_inc(hact_ready, 1)
                if not last:
                    route(m + 1, (m + 1) * per_route)
                v.wait_ge(y_cleared, m + 2)
                v.wait_ge(hact_ready, m + 1)
                v.nop(nofuse=True)
                with v.Fori(0, HK // RING) as r:
                    for s in range(RING):
                        v.wait_ge(gathered[s], m * (32 * (HK // RING)) + r * 16 + 16 * (HK // RING + 1))
                        v.wait_ge(tile_used, m * 2 * HK + r * RING + (RING + HK + s))
                        v.scalar_tensor_tensor(out=y_ps, in0=ring[:, s, :], scalar=hact[:, bass.ds(r * RING + s, 1)],
                                               in1=y_ps, op0=ALU.mult, op1=ALU.add).then_inc(tile_used, 1)
                v.wait_ge(tile_used, m * 2 * HK + (RING + 2 * HK))
                hm = XH[:, bass.ds(m, 1), :].rearrange("p a n -> p (a n)")
                v.tensor_tensor(hm, y_ps, hm, ALU.add).then_inc(y_added, 1)
                v.wait_ge(fin_sq, m + 1)
                mean_square(stat[:, 0:1], stat[:, 1:2]).then_inc(fin_ms, 1)
                v.wait_ge(fin_std, m + 1)
                v.reciprocal(stat[:, 3:4], stat[:, 2:3]).then_inc(fin_step, 1)
                v.wait_ge(fin_step, m + 1)
                v.wait_ge(gfin_loaded, 16)
                v.scalar_tensor_tensor(out=hm, in0=hm, scalar=stat[:, 3:4], in1=gfin[:, :], op0=ALU.mult,
                                       op1=ALU.mult).then_inc(out_ready, 1)

            v.wait_ge(topk_step, RANK_STEPS * 2 * PH)
            v.sem_inc(y_cleared, 1)
            v.sem_inc(tile_used, RING)
            per_route = route(0, 0)
            with v.Fori(0, TB - 1) as m:
                experts(m, False, per_route)
            experts(TB - 1, True, per_route)

    return nc


_INS = ["x", "norm_mix_g", "w_in", "conv_dw_w", "conv_dw_b", "conv_ln_g", "conv_ln_b", "w_conv_out", "attn_sinks",
        "w_attn_out", "w_out", "norm_ffn_g", "peer_w_q", "peer_sub_keys", "peer_u", "peer_v", "final_norm_g"]


def kernel(**inputs):
    import concourse.bacc as bacc
    from concourse.bass_utils import run_bass_kernel_spmd

    nc = bacc.Bacc("TRN2", target_bir_lowering=False, num_devices=1)
    arrays, args = {}, []
    for name in _INS:
        a = np.ascontiguousarray(inputs[name])
        arrays[f"in_{name}"] = a
        args.append(nc.dram_tensor(f"in_{name}", a.shape, mybir.dt.from_np(a.dtype), kind="ExternalInput").ap())
    shape = arrays["in_x"].shape
    args.append(nc.dram_tensor("out_h", shape, F32, kind="ExternalOutput").ap())
    build(nc, *args)
    r = run_bass_kernel_spmd(nc, [arrays], core_ids=[0])
    return r.results[0]["out_h"]
```

```python
from contextlib import ExitStack

import numpy as np

import concourse.bass as bass
from concourse import mybir

F32 = mybir.dt.float32
F32R = mybir.dt.float32r
U32 = mybir.dt.uint32
I32 = mybir.dt.int32
ALU = mybir.AluOpType
ACT = mybir.ActivationFunctionType
AX = mybir.AxisListType

P = 128
T = 512
TB = T // P
D = 2048
KD = D // P
CONV = 1024
CC = CONV // P
TAPS = 31
PAD = TAPS - 1
NQ, NKV, HD = 16, 2, 64
QDIM = NQ * HD
Q0 = 2 * CONV
K0 = Q0 + QDIM
V0 = K0 + NKV * HD
G0 = V0 + NKV * HD
CHUNK = 64
PH = 8
NK = 128
TOPK = 16
HK = PH * TOPK
RMS_EPS = 1e-6
LN_EPS = 1e-5
MASKED = -3.0e38
UK, UC = 8, 256
RING = 8
RANK_STEPS = 5 * TB + 2
HEAD_STEPS = 14
HG = 4
SLOPES = [float(np.float32(np.power(np.float32(2.0), np.float32(-8.0 * (h + 1) / NQ)))) for h in range(NQ)]

U_Q = 0
U_KV = U_Q + 8
U_GLU = U_KV + 2
U_MIX = U_GLU + 16
MIX_IT = D // (2 * UC)
U_OUT = U_MIX + 2 * 6 * MIX_IT
U_PQ = U_OUT + 16
S_MIX = U_MIX
S_OUT = S_MIX + 2 * 4 * MIX_IT
S_PQ = S_OUT + 16

FREE, FULL = {}, {}


def _count_banks():
    free, full = [0] * 8, [0] * 8
    steps = [
        ("xT", [4, 4, 4, 4, 1, 0, 0, 0], [4, 4, 4, 4, 1, 0, 0, 0]),
        ("q", [2, 2, 2, 2, 0, 0, 0, 0], [0] * 8),
        ("kv", [1, 1, 0, 0, 0, 0, 0, 0], [0] * 8),
        ("kdup", [0, 0, 1, 1, 0, 0, 0, 0], [0, 0, 1, 1, 0, 0, 0, 0]),
        ("vtok", [1, 0, 0, 0, 0, 0, 0, 0], [1, 0, 0, 0, 0, 0, 0, 0]),
        ("glu", [4, 4, 4, 4, 0, 0, 0, 0], [0] * 8),
        ("attn", [0, 0, 0, 0, 16, 16, 32, 16], [0, 0, 0, 0, 16, 16, 32, 16]),
        ("mixA", [4] * 8, [0] * 8),
        ("ln", [0, 0, 0, 0, 1, 1, 0, 0], [0, 0, 0, 0, 1, 0, 0, 0]),
        ("mixB", [4] * 8, [0] * 8),
        ("out", [4] * 8, [0] * 8),
        ("xnT", [4, 4, 4, 4, 0, 0, 0, 0], [4, 4, 4, 4, 0, 0, 0, 0]),
        ("keys", [0, 0, 0, 0, 1, 1, 1, 1], [0, 0, 0, 0, 1, 1, 1, 1]),
        ("pq", [4] * 8, [0, 0, 0, 0, 4, 4, 4, 4]),
        ("end", [0] * 8, [0] * 8),
    ]
    for name, given_back, filled in steps:
        FREE[name], FULL[name] = list(free), list(full)
        free = [a + b for a, b in zip(free, given_back)]
        full = [a + b for a, b in zip(full, filled)]


_count_banks()


def build(nc, x, norm_mix_g, w_in, conv_dw_w, conv_dw_b, conv_ln_g, conv_ln_b, w_conv_out, attn_sinks,
          w_attn_out, w_out, norm_ffn_g, peer_w_q, peer_sub_keys, peer_u, peer_v, final_norm_g, out):
    ctx = ExitStack()
    with ctx:
        def sb(name, shape, dt=F32, stack=ctx):
            return stack.enter_context(nc.sbuf_tensor(name, shape, dt))

        def sem(name):
            return ctx.enter_context(nc.semaphore(name))

        ident = sb("ident", [P, P])
        lnmean = sb("lnmean", [P, P])
        negdist = sb("negdist", [P, 2 * P])
        disti = sb("disti", [P, 2 * P], I32)
        vecs = sb("vecs", [P, 56 + 8 * TAPS])
        sinks = sb("sinks", [P, NQ])
        stat = sb("stat", [P, 16])
        soft = sb("soft", [P, 2, 6, HG])
        iota16i = sb("iota16i", [P, TOPK], I32)
        iota16 = sb("iota16", [P, TOPK])
        XH = sb("XH", [P, TB, D])
        B = sb("B", [P, CC * (T + PAD) + QDIM // P * T])
        G = sb("G", [P, 6400])
        g1T, g2T = vecs[:, 0:16], vecs[:, 40:56]
        cbT, lgT, lbT = vecs[:, 16:24], vecs[:, 24:32], vecs[:, 32:40]
        cwT = vecs[:, 56:56 + 8 * TAPS].rearrange("p (t c) -> p t c", c=CC)
        xhf = XH[:, :, :].rearrange("p m n -> p (m n)")
        mixT = xhf.rearrange("p (k t) -> p k t", t=T)
        qT = xhf[:, 0:4096].rearrange("p (c t) -> p c t", t=T)
        kT = xhf[:, 4096:5120].rearrange("p (g t) -> p g t", g=NKV)
        vtok = xhf[:, 5120:5632].rearrange("p (m d) -> p m d", d=P)
        Sc = xhf[:, 5632:7680].rearrange("p (b h s) -> p b h s", b=2, h=HG)
        uT = B[:, 0:CC * (T + PAD)].rearrange("p (c t) -> p c t", c=CC)
        OT = B[:, CC * (T + PAD):].rearrange("p (c t) -> p c t", t=T)
        g2b, gfin, squares = B[:, 0:D], B[:, D:2 * D], B[:, 2 * D:3 * D]
        idx = B[:, 6144:6656].bitcast(U32).rearrange("p (m k) -> p m k", m=TB)
        cand = B[:, 6656:6912].rearrange("p (a b) -> p a b", b=TOPK)
        cand2 = B[:, 6912:7168]
        pick = B[:, 7168:7680].rearrange("p (s a b) -> p s a b", s=2, b=TOPK)
        tops = B[:, 7680:7808].rearrange("p (h k) -> p h k", h=PH)
        sumv, sumi = B[:, 7808:7824], B[:, 7824:7840].bitcast(U32)
        sump = B[:, 7840:7872].bitcast(U32).rearrange("p (s k) -> p s k", s=2)
        sumf = B[:, 7872:7904].rearrange("p (s k) -> p s k", s=2)
        isel = B[:, 7904:7936].rearrange("p (s k) -> p s k", s=2)
        PT = G[:, 0:2048].rearrange("p (b h s t) -> p b h s t", b=2, h=HG, s=2)
        qblk = G[:, 2048:3072].rearrange("p (c t) -> p c t", t=P)
        vblk = G[:, 3072:3328].rearrange("p (s d) -> p s d", s=2)
        acc = G[:, 3328:4352].rearrange("p (b t) -> p b t", b=2)
        kblk = G[:, 3840:4352].rearrange("p (g t) -> p g t", g=NKV)
        mu = G[:, 4352:4864]
        rstd = G[:, 4864:5376]
        sq = G[:, 5376:6400].rearrange("p (b t) -> p b t", b=2)
        vrows = G[:, 5376:5760].rearrange("p (r n) -> p r n", n=P)
        kvT = G[:, 4352:5376].rearrange("p (b t) -> p b t", b=2)
        sig = G[:, 0:2048].rearrange("p (b t) -> p b t", t=T)
        glusig = sq
        skT = G[:, 0:2048].rearrange("p (i n) -> p i n", n=NK)
        skraw = G[:, 2048:4096].rearrange("p (i d) -> p i d", d=P)
        qchunk = G[:, 2048:3072].rearrange("p (b t) -> p b t", b=2)
        sc = G[:, 3072:3584].rearrange("p (m n) -> p m n", m=TB)
        topv = G[:, 4096:5120].rearrange("p (m i k) -> p m i k", m=TB, i=2 * PH)
        topi = G[:, 5120:6144].rearrange("p (m i k) -> p m i k", m=TB, i=2 * PH)
        bestv = G[:, 3584:3648].rearrange("p (m k) -> p m k", m=TB)
        besti = G[:, 3648:3712].bitcast(U32).rearrange("p (m k) -> p m k", m=TB)

        early = ExitStack()
        aTh = sb("aTh", [P, KD, T], F32R, early)
        aTl = sb("aTl", [P, KD, T], F32R, early)
        Wh = sb("Wh", [P, 2, UK, UC], F32R, early)
        Wl = sb("Wl", [P, 2, UK, UC], F32R, early)
        raw = sb("raw", [P, 2, UK, UC], F32, early)
        early.close()
        ring = sb("ring", [P, RING, D])
        rs = sb("rs", [P, 2, PH])
        gates = sb("gates", [P, HK])
        idxs = sb("idxs", [P, 2 * RING], U32)
        hid = sb("hid", [P, HK])
        hact = sb("hact", [P, HK])

        PS = ctx.enter_context(nc.psum_tensor("PS", [P, 8, T], F32))
        xn_ps = PS[:, 0:4, :].rearrange("p b t -> p (b t)")
        y_ps = PS[:, 4:8, :].rearrange("p b t -> p (b t)")

        w_loaded = [sem("w_loaded0"), sem("w_loaded1")]
        hi_done, lo_done = sem("hi_done"), sem("lo_done")
        halves = sem("halves")
        full = [sem(f"bank_full{b}") for b in range(8)]
        free = [sem(f"bank_free{b}") for b in range(8)]
        x_loaded = [sem(f"x_loaded{m}") for m in range(TB)]
        consts_loaded, keys_loaded, x_reloaded = (sem(n) for n in ("consts_loaded", "keys_loaded", "x_reloaded"))
        pool_const, dve_const = sem("pool_const"), sem("dve_const")
        squares_done, meansq_done, std_done, inv_done, norm_done = (
            sem(n) for n in ("squares_done", "meansq_done", "std_done", "inv_done", "norm_done"))
        aT_hi, aT_lo = sem("aT_hi"), sem("aT_lo")
        glu_done, conv_step = sem("glu_done"), sem("conv_step")
        centred, squared, sq_used, var_ready, lnstd_done, ln_step, u_ready = (
            sem(n) for n in ("centred", "squared", "sq_used", "var_ready", "lnstd_done", "ln_step", "u_ready"))
        blk_staged = sem("blk_staged")
        attn_step, negmax_ready, exp_done, p_ready = (
            sem(n) for n in ("attn_step", "negmax_ready", "exp_done", "p_ready"))
        mix_ready = sem("mix_ready")
        rank_step, head_step, gate_step, sub_ready, gexp_done, idx_ready = (
            sem(n) for n in ("rank_step", "head_step", "gate_step", "sub_ready", "gexp_done", "idx_ready"))
        staged = sem("staged")
        gathered = [sem(f"gathered{s}") for s in range(RING)]
        tile_used = sem("tile_used")
        y_cleared = sem("y_cleared")
        xn_in_psum, gelu_done, hact_ready = sem("xn_in_psum"), sem("gelu_done"), sem("hact_ready")
        y_added, fin_sq, fin_ms, fin_std, fin_step, out_ready, stored = (
            sem(n) for n in ("y_added", "fin_sq", "fin_ms", "fin_std", "fin_step", "out_ready", "stored"))

        block = ctx.enter_context(nc.Block())

        @block.sync
        def _(sp):
            xt = x[0].rearrange("(m p) n -> p m n", p=P)
            for m in range(TB):
                sp.dma_start(XH[:, m, :], xt[:, m, :]).then_inc(x_loaded[m], 16)
            rows = [norm_mix_g[0].rearrange("(k p) -> k p", p=P), conv_dw_b[0].rearrange("(k p) -> k p", p=P),
                    conv_ln_g[0].rearrange("(k p) -> k p", p=P), conv_ln_b[0].rearrange("(k p) -> k p", p=P),
                    norm_ffn_g[0].rearrange("(k p) -> k p", p=P)]
            at = 0
            for r in rows:
                sp.dma_start(vrows[at:at + r.shape[0], 0, :], r).then_inc(consts_loaded, 16)
                at += r.shape[0]
            cw = conv_dw_w[0].rearrange("t (c p) -> (t c) p", p=P)
            half = 4 * TAPS
            for j in range(2):
                sp.dma_start(vrows[0:half, 1 + j, :], cw[j * half:(j + 1) * half, :]).then_inc(consts_loaded, 16)
            sp.dma_start(sinks[:, :], attn_sinks[0:1, :].to_broadcast([P, NQ])).then_inc(consts_loaded, 16)

            def load(src, k0, c0, slot):
                sp.nop(nofuse=True)
                view = src[k0 * P:(k0 + UK) * P, :].rearrange("(k p) n -> p k n", p=P)
                sp.dma_start(raw[:, slot, :, :], view[:, :, bass.ds(c0, UC)]).then_inc(w_loaded[slot], 16)

            def q_units(it):
                for u in range(4):
                    if it or u >= 2:
                        sp.wait_ge(lo_done, 4 * it + u - 1)
                    load(w_in[0], (u % 2) * UK, it * 2 * UC + Q0 + u // 2 * UC, u % 2)

            q_units(0)
            q_units(1)
            for u in range(2):
                sp.wait_ge(lo_done, U_KV + u - 1)
                load(w_in[0], u * UK, K0, u)
            with sp.Fori(0, 4) as g:
                for u in range(4):
                    sp.wait_ge(lo_done, g * 4 + (U_GLU + u - 1))
                    load(w_in[0], (u % 2) * UK, g * UC + (CONV if u < 2 else 0), u % 2)

            for branch, gate0, w_branch in ((0, G0 + D, w_attn_out), (1, G0, w_conv_out)):
                with sp.Fori(0, MIX_IT) as g:
                    n0, s0 = U_MIX + 6 * MIX_IT * branch, S_MIX + 4 * MIX_IT * branch
                    for u in range(6):
                        if u < 2:
                            sp.wait_ge(halves, g * 12 + 2 * (n0 + u - 1))
                        else:
                            sp.wait_ge(lo_done, g * 4 + (s0 + u - 1))
                        if u < 4:
                            load(w_in[0], (u % 2) * UK, g * 2 * UC + (gate0 + u // 2 * UC), u % 2)
                        else:
                            load(w_branch[0], 0, g * 2 * UC + (u % 2) * UC, u % 2)

            def out_units(it, first):
                for u in range(4):
                    if first and u < 2:
                        sp.wait_ge(halves, 2 * (U_OUT + u - 1))
                    else:
                        sp.wait_ge(lo_done, it * 4 + (S_OUT + u - 1))
                    load(w_out[0], (u % 2) * UK, it * 2 * UC + (u // 2) * UC, u % 2)

            out_units(0, True)
            sp.dma_start(g2b, norm_ffn_g[0:1, :].to_broadcast([P, D])).then_inc(keys_loaded, 16)
            sp.dma_start(gfin, final_norm_g.rearrange("(a n) -> a n", a=1).to_broadcast([P, D])).then_inc(keys_loaded, 16)
            with sp.Fori(1, 4) as it:
                out_units(it, False)
            sp.dma_start(skraw, peer_sub_keys[0].rearrange("h s n d -> n (h s) d")).then_inc(keys_loaded, 16)
            with sp.Fori(0, 4) as it:
                for u in range(4):
                    sp.wait_ge(lo_done, it * 4 + (S_PQ + u - 1))
                    load(peer_w_q[0], (u % 2) * UK, it * 2 * UC + (u // 2) * UC, u % 2)
            ot = out[0].rearrange("(m p) n -> p m n", p=P)
            with sp.Fori(0, TB) as m:
                sp.wait_ge(out_ready, m + 1)
                sp.dma_start(ot[:, bass.ds(m, 1), :], XH[:, bass.ds(m, 1), :]).then_inc(stored, 16)
            sp.wait_ge(stored, 16 * TB)


        @block.gpsimd
        def _(pool):
            pool.memset(ident[:, :], 0.0).then_inc(pool_const, 1)
            pool.wait_ge(pool_const, 1)
            pool.affine_select(out=ident[:, :], in_=ident[:, :], compare_op=ALU.not_equal, fill=1.0,
                               base=0, pattern=[[-1, P]], channel_multiplier=1).then_inc(pool_const, 1)
            pool.iota(disti[:, :], pattern=[[-1, 2 * P]], base=P, channel_multiplier=1).then_inc(pool_const, 1)
            pool.iota(iota16i[:, :], pattern=[[1, TOPK]], base=0, channel_multiplier=0).then_inc(pool_const, 1)

            def stage(m, first):
                if first:
                    for b in range(4):
                        pool.wait_ge(free[b], FREE["glu"][b])
                    pool.tensor_copy(qblk, qT[:, :, 0:P]).then_inc(blk_staged, 1)
                    pool.tensor_copy(kblk[:, :, P:], kT[:, :, 0:P]).then_inc(blk_staged, 1)
                    pool.tensor_copy(vblk[:, 1, :], vtok[:, 0, :]).then_inc(blk_staged, 1)
                else:
                    pool.wait_ge(full[5], m * 4 + FULL["attn"][5])
                    pool.wait_ge(full[6], m * 8 + FULL["attn"][6])
                    pool.tensor_copy(qblk, qT[:, :, bass.ds(m * P, P)]).then_inc(blk_staged, 1)
                    pool.tensor_copy(kblk, kT[:, :, bass.ds((m - 1) * P, 2 * P)]).then_inc(blk_staged, 1)
                    pool.tensor_copy(vblk, vtok[:, bass.ds(m - 1, 2), :]).then_inc(blk_staged, 1)

            stage(0, True)
            with pool.Fori(1, TB) as m:
                stage(m, False)

            rounds = HK // (2 * RING)
            with pool.Fori(0, TB) as m:
                pool.wait_ge(idx_ready, m * PH + PH)
                pool.nop(nofuse=True)
                for part, table in enumerate((peer_u, peer_v)):
                    with pool.Fori(0, rounds) as r:
                        for h in range(2):
                            pool.tensor_copy(idxs[:, h * RING:(h + 1) * RING],
                                             idx[:, bass.ds(m, 1), bass.ds(r * 2 * RING + h * RING, RING)]
                                             .rearrange("p a k -> p (a k)")).then_inc(staged, 1)
                            pool.wait_ge(staged, m * (4 * rounds) + r * 2 + (part * 2 * rounds + h + 1))
                            for s in range(RING):
                                pool.wait_ge(tile_used, m * 2 * HK + r * 2 * RING + (part * HK + h * RING + s + 1))
                                pool.nop(nofuse=True)
                                pool.indirect_dma_start(
                                    ring[:, s, :], None, table[0],
                                    bass.IndirectOffsetOnAxis(idxs[:, h * RING + s:h * RING + s + 1], 0),
                                ).then_inc(gathered[s], 16)

        @block.scalar
        def _(act):
            for m in range(TB):
                act.wait_ge(x_loaded[m], 16)
                act.activation(aTl[:, 4 * m:4 * m + 4, :].rearrange("p k t -> p (k t)"), XH[:, m, :], ACT.Square,
                               accum_out=stat[:, m:m + 1]).then_inc(squares_done, 1)
            act.wait_ge(meansq_done, 1)
            act.activation(stat[:, 8:12], stat[:, 4:8], ACT.Sqrt).then_inc(std_done, 1)
            act.wait_ge(inv_done, 1)
            for m in (2, 3):
                act.activation(XH[:, m, :], XH[:, m, :], ACT.Copy, scale=stat[:, 12 + m:13 + m]).then_inc(norm_done, 1)
            act.wait_ge(full[4], 1)
            act.activation(vecs[:, :], PS[:, 4, 0:56 + 8 * TAPS], ACT.Copy).then_inc(free[4], 1)
            act.wait_ge(free[4], 1)
            for k in range(KD):
                act.wait_ge(full[k % 4], k // 4 + 1)
                act.activation(aTh[:, k, :], PS[:, k % 4, :], ACT.Copy, scale=g1T[:, k:k + 1]).then_inc(aT_hi, 1)

            def hi(n, slot, loads, first=False):
                act.wait_ge(w_loaded[slot], loads)
                if not first:
                    act.wait_ge(halves, n * 2 - 2)
                act.activation(Wh[:, slot, :, :], raw[:, slot, :, :], ACT.Copy).then_inc(hi_done, 1)

            def hi4(it, base, u):
                hi(it * 4 + (base + u), u % 2, it * 32 + 16 * ((base + u) // 2 + 1))

            hi(0, 0, 16, True)
            for it in range(2):
                for u in range(4):
                    n = it * 4 + u + 1
                    hi(n, n % 2, 16 * (n // 2 + 1), n < 2)
                    if u % 2:
                        act.wait_ge(halves, 2 * n)
                        for b in range(2):
                            act.activation(qT[:, it * 4 + u // 2 * 2 + b, :], PS[:, u // 2 * 2 + b, :], ACT.Copy,
                                           scale=HD ** -0.5).then_inc(free[u // 2 * 2 + b], 1)
            hi4(0, U_KV, 1)
            hi4(0, U_KV, 2)
            act.wait_ge(halves, 2 * U_GLU)
            for b in range(2):
                act.activation(kvT[:, b, :], PS[:, b, :], ACT.Copy).then_inc(free[b], 1)
            for b in (2, 3):
                act.wait_ge(full[b], FULL["kdup"][b] + 1)
                act.activation(kT[:, b - 2, :], PS[:, b, :], ACT.Copy).then_inc(free[b], 1)
            act.wait_ge(full[0], FULL["vtok"][0] + 1)
            act.activation(vtok, PS[:, 0, :].rearrange("p (m d) -> p m d", m=TB), ACT.Copy).then_inc(free[0], 1)

            def glu_attn(g, first):
                lo = P if first else 0

                def exps(hg):
                    b = hg % 2
                    act.wait_ge(negmax_ready, g * 4 + (hg + 1))
                    for i in range(HG):
                        act.activation(Sc[:, b, i, lo:], Sc[:, b, i, lo:], ACT.Exp, bias=soft[:, b, 1, i:i + 1],
                                       accum_out=soft[:, b, 2, i:i + 1])
                    act.activation(soft[:, b, 4, :], soft[:, b, 3, :], ACT.Exp).then_inc(exp_done, 1)

                def pt_copy(hg):
                    if not (first and hg < 2):
                        act.wait_ge(full[6], g * 8 + (FULL["attn"][6] + 2 * hg - 2))
                    for j in range(2):
                        act.wait_ge(full[6 + j], g * (8 - 4 * j) + (FULL["attn"][6 + j] + (2 - j) * hg + 1))
                        act.activation(PT[:, hg % 2, 2 * j:2 * j + 2, lo // P:, :],
                                       PS[:, 6 + j, :].rearrange("p (h s t) -> p h s t", h=2, s=2)[:, :, lo // P:, :],
                                       ACT.Copy).then_inc(free[6 + j], 1)

                def o_copy(hg):
                    act.wait_ge(full[6], g * 8 + (FULL["attn"][6] + 2 * hg + 2))
                    act.activation(OT[:, 2 * hg:2 * hg + 2, bass.ds(g * P, P)],
                                   PS[:, 6, 0:2 * P].rearrange("p (c t) -> p c t", c=2), ACT.Copy).then_inc(free[6], 1)

                hi4(g, U_GLU, 1)
                hi4(g, U_GLU, 2)
                exps(0)
                exps(1)
                hi4(g, U_GLU, 3)
                pt_copy(0)
                o_copy(0)
                if not first:
                    act.wait_ge(glu_done, g * 2)
                for b in range(2):
                    act.activation(glusig[:, b, :], PS[:, b, :], ACT.Sigmoid).then_inc(free[b], 1)
                exps(2)
                hi4(g, U_GLU, 4)
                pt_copy(1)
                o_copy(1)
                exps(3)
                pt_copy(2)
                o_copy(2)
                pt_copy(3)
                o_copy(3)

            glu_attn(0, True)
            with act.Fori(1, 4) as g:
                glu_attn(g, False)

            def mix(branch, g, ln):
                n0 = U_MIX + 6 * MIX_IT * branch

                def mix_hi(u):
                    hi(g * 6 + (n0 + u), u % 2, g * 48 + 16 * ((n0 + u) // 2 + 1))

                def sigmoids(first_bank, u):
                    act.wait_ge(halves, g * 12 + 2 * (n0 + u + 1))
                    for b in (first_bank, first_bank + 1):
                        act.activation(sig[:, b, :], PS[:, b, :], ACT.Sigmoid).then_inc(free[b], 1)

                mix_hi(1)
                mix_hi(2)
                if ln:
                    act.wait_ge(full[4], FULL["ln"][4] + 1)
                    act.activation(mu, PS[:, 4, :], ACT.Copy).then_inc(free[4], 1)
                    for c in range(CC):
                        act.wait_ge(centred, c + 1)
                        if c >= 2:
                            act.wait_ge(sq_used, c - 1)
                        act.activation(sq[:, c % 2, :], uT[:, c, 0:T], ACT.Square).then_inc(squared, 1)
                act.wait_ge(mix_ready, g * 4 + (4 * MIX_IT * branch + 1))
                sigmoids(0, 1)
                mix_hi(3)
                if ln:
                    act.wait_ge(free[5], FREE["ln"][5] + 1)
                    act.activation(rstd, rstd, ACT.Sqrt).then_inc(lnstd_done, 1)
                    for c in range(CC):
                        act.wait_ge(ln_step, 2 + c)
                        act.activation(uT[:, c, 0:T], uT[:, c, 0:T], ACT.Silu, bias=lbT[:, c:c + 1],
                                       scale=lgT[:, c:c + 1]).then_inc(u_ready, 1)
                sigmoids(2, 3)
                mix_hi(6)

            with act.Fori(0, MIX_IT) as g:
                mix(0, g, False)
            mix(1, 0, True)
            with act.Fori(1, MIX_IT) as g:
                mix(1, g, False)

            act.wait_ge(mix_ready, 8 * MIX_IT + 1)
            for k in range(4):
                act.activation(aTh[:, 4 * k:4 * k + 4, :], mixT[:, 4 * k:4 * k + 4, :], ACT.Copy).then_inc(aT_hi, 1)
            act.wait_ge(aT_lo, 4)
            act.dma_start(XH[:, :, :], x[0].rearrange("(m p) n -> p m n", p=P)).then_inc(x_reloaded, 16)
            with act.Fori(0, 4) as it:
                for u in range(4):
                    hi4(it, U_OUT, u + 1)

            for k in range(KD):
                act.wait_ge(full[k % 4], FULL["xnT"][k % 4] + k // 4 + 1)
                act.activation(aTh[:, k, :], PS[:, k % 4, :], ACT.Copy, scale=g2T[:, k:k + 1]).then_inc(aT_hi, 1)
            for b in range(4, 8):
                act.wait_ge(full[b], FULL["keys"][b] + 1)
                act.activation(skT[:, 4 * b - 16:4 * b - 12, :], PS[:, b, :].rearrange("p (i n) -> p i n", i=4),
                               ACT.Copy).then_inc(free[b], 1)
            for m in range(TB):
                act.wait_ge(squares_done, TB + m)
                act.activation(squares, XH[:, m, :], ACT.Square, accum_out=stat[:, m:m + 1]).then_inc(squares_done, 1)
            act.wait_ge(meansq_done, 2)
            act.activation(stat[:, 8:12], stat[:, 4:8], ACT.Sqrt).then_inc(std_done, 1)

            def peer_q(it, last):
                for u in range(4):
                    if not (last and u == 3):
                        hi4(it, U_PQ, u + 1)
                    if u % 2:
                        act.wait_ge(halves, it * 8 + 2 * (U_PQ + u + 1))
                        for b in range(2):
                            last_bank = 6 + b if u == 1 else 4 + b
                            act.wait_ge(full[last_bank], it + (FULL["pq"][last_bank] + u // 2))
                            act.activation(qchunk[:, b, :], PS[:, u // 2 * 2 + b, :], ACT.Copy)\
                               .then_inc(free[u // 2 * 2 + b], 1)

            with act.Fori(0, 3) as it:
                peer_q(it, False)
            peer_q(3, True)

            def gate_exp(m):
                act.wait_ge(sub_ready, m + 1)
                act.activation(tops, tops, ACT.Exp).then_inc(gexp_done, 1)

            def experts(m, last):
                act.wait_ge(y_cleared, m + 1)
                act.activation(hact[:, :], hid[:, :], ACT.Gelu_apprx_tanh).then_inc(gelu_done, 1)
                if not last:
                    gate_exp(m + 1)
                act.wait_ge(y_added, m + 1)
                act.activation(squares, XH[:, bass.ds(m, 1), :].rearrange("p a n -> p (a n)"), ACT.Square,
                               accum_out=stat[:, 0:1]).then_inc(fin_sq, 1)
                act.wait_ge(fin_ms, m + 1)
                act.activation(stat[:, 2:3], stat[:, 1:2], ACT.Sqrt).then_inc(fin_std, 1)

            gate_exp(0)
            with act.Fori(0, TB - 1) as m:
                experts(m, False)
            experts(TB - 1, True)

        @block.tensor
        def _(pe):
            pe.wait_ge(pool_const, 4)
            pe.wait_ge(consts_loaded, 16 * 8)
            half = 4 * TAPS
            pe.transpose(PS[:, 4, 0:56], vrows[0:56, 0, :], ident[0:56, 0:56])
            for j in range(2):
                ins = pe.transpose(PS[:, 4, 56 + j * half:56 + (j + 1) * half], vrows[0:half, 1 + j, :], ident[0:half, 0:half])
            ins.then_inc(full[4], 1)

            def to_xT(src, phase):
                for k in range(KD):
                    if FREE[phase][k % 4] + k // 4:
                        pe.wait_ge(free[k % 4], FREE[phase][k % 4] + k // 4)
                    for m in range(TB):
                        ins = pe.transpose(PS[:, k % 4, m * P:(m + 1) * P], src[:, m, k * P:(k + 1) * P], ident[:, :])
                    ins.then_inc(full[k % 4], 1)

            pe.wait_ge(norm_done, TB)
            to_xT(XH, "xT")

            def unit(split, slot, bank, start, stop, k0):
                pe.wait_ge(lo_done, split)
                for b in range(2):
                    for k in range(UK):
                        for j, (w, a) in enumerate(((Wh, aTh), (Wl, aTh), (Wh, aTl))):
                            ins = pe.matmul(PS[:, bank + b, :], w[:, slot, k, b * P:(b + 1) * P], a[:, k0 + k, :],
                                            start=start and k == 0 and j == 0, stop=stop and k == UK - 1 and j == 2)
                    ins.then_inc(halves, 1)

            def group(split, bank, it, phase):
                for b in range(2):
                    pe.wait_ge(free[bank + b], it + FREE[phase][bank + b])
                unit(split, 0, bank, True, False, 0)
                unit(split + 1, 1, bank, False, True, UK)

            for it in range(2):
                group(it * 4 + 1, 0, it, "q")
                group(it * 4 + 3, 2, it, "q")
            group(U_KV + 1, 0, 0, "kv")
            pe.wait_ge(free[0], FREE["kv"][0] + 1)
            for g in range(NKV):
                pe.wait_ge(free[2 + g], FREE["kdup"][2 + g])
                for b in range(2):
                    ins = pe.matmul(PS[b * HD:(b + 1) * HD, 2 + g, :], ident[:, g * HD:(g + 1) * HD], kvT[:, 0, :],
                                    start=True, stop=True)
                ins.then_inc(full[2 + g], 1)
            pe.wait_ge(free[1], FREE["kv"][1] + 1)
            for m in range(TB):
                ins = pe.transpose(PS[:, 0, m * P:(m + 1) * P], kvT[:, 1, m * P:(m + 1) * P], ident[:, :])
            ins.then_inc(full[0], 1)

            def glu_attn(g, first):
                parts = (1,) if first else (0, 1)

                def qk(hg):
                    for i in range(HG):
                        h, bank = HG * hg + i, 4 + i % 2
                        o = (h % 2) * HD
                        if i < 2:
                            pe.wait_ge(free[bank], g * 4 + (FREE["attn"][bank] + hg))
                        at, lo = (i // 2) * 2 * P, P if first else 0
                        ins = pe.matmul(PS[:, bank, at + lo:at + 2 * P], qblk[o:o + HD, h // 2, :],
                                        kblk[o:o + HD, h // PH, lo:], start=True, stop=True)
                        if i >= 2:
                            ins.then_inc(full[bank], 1)

                def transposes(hg):
                    pe.wait_ge(p_ready, g * 4 + (hg + 1))
                    for i in range(HG):
                        bank = 6 + i // 2
                        if i % 2 == 0 and not (first and hg == 0):
                            pe.wait_ge(free[bank], g * (8 if bank == 6 else 4) + (FREE["attn"][bank] + (2 if bank == 6 else 1) * hg))
                        for s in parts:
                            at = (i % 2) * 2 * P + s * P
                            ins = pe.transpose(PS[:, bank, at:at + P], Sc[:, hg % 2, i, s * P:(s + 1) * P], ident[:, :])
                        if i % 2:
                            ins.then_inc(full[bank], 1)

                def pv(hg):
                    pe.wait_ge(free[6], g * 8 + (FREE["attn"][6] + 2 * hg + 1))
                    pe.wait_ge(free[7], g * 4 + (FREE["attn"][7] + hg + 1))
                    for i in range(HG):
                        h = HG * hg + i
                        o = (h % 2) * HD
                        for s in parts:
                            ins = pe.matmul(PS[o:o + HD, 6, i // 2 * P:(i // 2 + 1) * P],
                                            vblk[:, s, h // PH * HD:(h // PH + 1) * HD], PT[:, hg % 2, i, s, :],
                                            start=s == parts[0], stop=s == 1)
                    ins.then_inc(full[6], 1)

                for b in range(2):
                    pe.wait_ge(free[b], g + FREE["glu"][b])
                unit(g * 4 + (U_GLU + 1), 0, 0, True, False, 0)
                pe.wait_ge(blk_staged, g * 3 + 3)
                qk(0)
                qk(1)
                unit(g * 4 + (U_GLU + 2), 1, 0, False, True, UK)
                transposes(0)
                qk(2)
                pv(0)
                for b in (2, 3):
                    pe.wait_ge(free[b], g + FREE["glu"][b])
                unit(g * 4 + (U_GLU + 3), 0, 2, True, False, 0)
                transposes(1)
                qk(3)
                pv(1)
                unit(g * 4 + (U_GLU + 4), 1, 2, False, True, UK)
                for hg in (2, 3):
                    transposes(hg)
                    pv(hg)

            glu_attn(0, True)
            with pe.Fori(1, 4) as g:
                glu_attn(g, False)

            def mix(branch, g, phase, ln):
                s0 = S_MIX + 4 * MIX_IT * branch
                for b in range(2):
                    pe.wait_ge(free[b], g + FREE[phase][b])
                unit(g * 4 + (s0 + 1), 0, 0, True, False, 0)
                if ln:
                    pe.wait_ge(conv_step, 1 + CC * TAPS)
                    pe.wait_ge(free[4], FREE["ln"][4])
                    pe.wait_ge(free[5], FREE["ln"][5])
                    for c in range(CC):
                        ins = pe.matmul(PS[:, 4, :], lnmean[:, :], uT[:, c, 0:T], start=c == 0, stop=c == CC - 1)
                    ins.then_inc(full[4], 1)
                unit(g * 4 + (s0 + 2), 1, 0, False, True, UK)
                if ln:
                    for c in range(CC):
                        pe.wait_ge(squared, c + 1)
                        pe.matmul(PS[:, 5, :], lnmean[:, :], sq[:, c % 2, :], start=c == 0, stop=c == CC - 1)\
                          .then_inc(sq_used, 1)
                group(g * 4 + (s0 + 3), 2, g, phase)
                if ln:
                    pe.wait_ge(u_ready, CC)
                for slot in range(2):
                    pe.wait_ge(w_loaded[slot], g * 48 + 16 * ((U_MIX + 6 * MIX_IT * branch) // 2 + 3))
                    for b in range(2):
                        bank = 4 + 2 * slot + b
                        pe.wait_ge(free[bank], g + FREE[phase][bank])
                        for k in range(UK):
                            ins = pe.matmul(PS[:, bank, :], raw[:, slot, k, b * P:(b + 1) * P],
                                            uT[:, k, 0:T] if branch else OT[:, k, :], start=k == 0, stop=k == UK - 1)
                        ins.then_inc(halves, 1)

            pe.wait_ge(free[6], FREE["mixA"][6])
            with pe.Fori(0, MIX_IT) as g:
                mix(0, g, "mixA", False)
            mix(1, 0, "mixB", True)
            with pe.Fori(1, MIX_IT) as g:
                mix(1, g, "mixB", False)

            with pe.Fori(0, 4) as it:
                for u in range(4):
                    pe.wait_ge(lo_done, it * 4 + (S_OUT + u + 1))
                    pe.wait_ge(aT_lo, 2 + 2 * (u % 2))
                    for m in range(TB):
                        bank = 4 * (u // 2) + m
                        if u % 2 == 0:
                            pe.wait_ge(free[bank], it + FREE["out"][bank])
                        for k in range(UK):
                            for j, (a, w) in enumerate(((aTh, Wh), (aTl, Wh), (aTh, Wl))):
                                ins = pe.matmul(PS[:, bank, 0:UC], a[:, (u % 2) * UK + k, m * P:(m + 1) * P],
                                                w[:, u % 2, k, :], start=u % 2 == 0 and k == 0 and j == 0,
                                                stop=u % 2 == 1 and k == UK - 1 and j == 2)
                        if m % 2:
                            ins.then_inc(halves, 1)

            for b in range(8):
                pe.wait_ge(free[b], FREE["xnT"][b])
            to_xT(XH, "xnT")
            pe.wait_ge(keys_loaded, 16 * 3)
            for b in range(4, 8):
                for i in range(4):
                    ins = pe.transpose(PS[:, b, i * P:(i + 1) * P], skraw[:, 4 * (b - 4) + i, :], ident[:, :])
                ins.then_inc(full[b], 1)

            def scores(it, gg):
                for b in range(2):
                    bank = 4 + 2 * gg + b
                    pe.wait_ge(free[bank], it + FREE["pq"][bank])
                    pe.wait_ge(free[2 * gg + b], it + (FREE["pq"][2 * gg + b] + 1))
                    for m in range(TB):
                        ins = pe.matmul(PS[:, bank, m * P:(m + 1) * P], qchunk[:, b, m * P:(m + 1) * P],
                                        skT[:, bass.ds(it * 4 + (2 * gg + b), 1), :].rearrange("p a n -> p (a n)"),
                                        start=True, stop=True)
                    ins.then_inc(full[bank], 1)

            def peer_q(it, first):
                for b in (0, 1):
                    pe.wait_ge(free[b], it + FREE["pq"][b])
                unit(it * 4 + (S_PQ + 1), 0, 0, True, False, 0)
                if not first:
                    scores(it - 1, 1)
                unit(it * 4 + (S_PQ + 2), 1, 0, False, True, UK)
                for b in (2, 3):
                    pe.wait_ge(free[b], it + FREE["pq"][b])
                unit(it * 4 + (S_PQ + 3), 0, 2, True, False, 0)
                scores(it, 0)
                unit(it * 4 + (S_PQ + 4), 1, 2, False, True, UK)

            peer_q(0, True)
            with pe.Fori(1, 4) as it:
                peer_q(it, False)
            scores(3, 1)

        @block.vector
        def _(v):
            class Steps:

                def __init__(self, s, base=0):
                    self.s, self.base, self.n = s, base, 0

                def did(self, ins):
                    ins.then_inc(self.s, 1)
                    self.n += 1

                def wait(self):
                    v.wait_ge(self.s, self.base + self.n)
                    v.nop(nofuse=True)

            consts = Steps(dve_const)
            consts.did(v.memset(lnmean[:, :], 1.0 / CONV))
            v.wait_ge(pool_const, 4)
            consts.did(v.tensor_copy(iota16[:, :], iota16i[:, :]))
            consts.did(v.tensor_copy(negdist[:, :], disti[:, :]))
            consts.wait()
            consts.did(v.scalar_tensor_tensor(out=negdist[:, :], in0=negdist[:, :], scalar=-1.0, in1=negdist[:, :],
                                              op0=ALU.mult, op1=ALU.min))
            consts.wait()
            consts.did(v.memset(negdist[0:CHUNK, 0:CHUNK], MASKED))
            consts.did(v.memset(negdist[0:CHUNK, 3 * CHUNK:], MASKED))
            consts.did(v.memset(negdist[CHUNK:, 0:2 * CHUNK], MASKED))
            v.sem_inc(mix_ready, 1)

            def mean_square(squares, out_):
                return v.tensor_scalar(out_, squares, 1.0 / D, RMS_EPS, ALU.mult, ALU.add)

            v.wait_ge(squares_done, TB)
            mean_square(stat[:, 0:4], stat[:, 4:8]).then_inc(meansq_done, 1)
            v.wait_ge(std_done, 1)
            v.reciprocal(stat[:, 12:16], stat[:, 8:12]).then_inc(inv_done, 1)
            v.wait_ge(inv_done, 1)
            for m in (0, 1):
                v.tensor_scalar(XH[:, m, :], XH[:, m, :], stat[:, 12 + m:13 + m], None, ALU.mult).then_inc(norm_done, 1)
            v.wait_ge(free[4], 1)
            for k in range(KD):
                v.wait_ge(aT_hi, k + 1)
                v.scalar_tensor_tensor(out=aTl[:, k, :], in0=PS[:, k % 4, :], scalar=g1T[:, k:k + 1],
                                       in1=aTh[:, k, :].bitcast(F32), op0=ALU.mult, op1=ALU.subtract)\
                 .then_inc(free[k % 4], 1)

            def lo(split, slot):
                v.wait_ge(hi_done, split)
                v.tensor_tensor(Wl[:, slot, :, :], raw[:, slot, :, :], Wh[:, slot, :, :].bitcast(F32), ALU.subtract)\
                 .then_inc(lo_done, 1)

            def conv(g, a, b):
                def one(ap):
                    return ap.rearrange("p a t -> p (a t)")
                for n in range(a, b):
                    k, j = n // 2, n % 2
                    tap, c = TAPS - 1 - k, bass.ds(g * 2 + j, 1)
                    src, w = one(uT[:, c, tap:tap + T]), cwT[:, tap, c]
                    if k == 0:
                        v.wait_ge(glu_done, g * 2 + (j + 1))
                    v.wait_ge(conv_step, g * (2 * TAPS) + max(n, 1))
                    if k == 0:
                        v.tensor_scalar(acc[:, j, :], src, w, cbT[:, c], ALU.mult, ALU.add).then_inc(conv_step, 1)
                    else:
                        v.scalar_tensor_tensor(out=one(uT[:, c, 0:T]) if k == TAPS - 1 else acc[:, j, :], in0=src,
                                               scalar=w, in1=acc[:, j, :], op0=ALU.mult, op1=ALU.add)\
                         .then_inc(conv_step, 1)

            v.memset(uT[:, :, 0:PAD], 0.0).then_inc(conv_step, 1)
            lo(1, 0)
            for n in range(U_GLU):
                lo(n + 2, (n + 1) % 2)
            v.wait_ge(consts_loaded, 16 * 8)

            def glu_attn(g, first, base):
                lo_ = P if first else 0
                steps = Steps(attn_step, base)

                def score(hg):
                    b = hg % 2
                    s_max, s_neg, _, s_sub, _, _ = (soft[:, b, j, :] for j in range(6))
                    if not (first and hg < 2):
                        v.wait_ge(full[7], g * 4 + (FULL["attn"][7] + hg - 1))
                    for i in range(HG):
                        bank, at = 4 + i % 2, (i // 2) * 2 * P
                        if i < 2:
                            v.wait_ge(full[bank], g * 4 + (FULL["attn"][bank] + hg + 1))
                        ins = v.scalar_tensor_tensor(out=Sc[:, b, i, lo_:], in0=negdist[:, lo_:],
                                                     scalar=SLOPES[HG * hg + i], in1=PS[:, bank, at + lo_:at + 2 * P],
                                                     op0=ALU.mult, op1=ALU.add)
                        if i >= 2:
                            ins.then_inc(free[bank], 1)
                        else:
                            steps.did(ins)
                    for bank in (4, 5):
                        v.wait_ge(free[bank], g * 4 + (FREE["attn"][bank] + hg + 1))
                    steps.wait()
                    steps.did(v.tensor_reduce(s_max, Sc[:, b, :, lo_:], AX.X, ALU.max))
                    steps.wait()
                    steps.did(v.tensor_tensor(s_max, s_max, sinks[:, HG * hg:HG * (hg + 1)], ALU.max))
                    steps.wait()
                    steps.did(v.tensor_scalar(s_neg, s_max, -1.0, None, ALU.mult))
                    v.tensor_tensor(s_sub, sinks[:, HG * hg:HG * (hg + 1)], s_max, ALU.subtract)\
                     .then_inc(negmax_ready, 1)

                def norm(hg):
                    b = hg % 2
                    s_sum, s_exp, s_inv = soft[:, b, 2, :], soft[:, b, 4, :], soft[:, b, 5, :]
                    v.wait_ge(exp_done, g * 4 + (hg + 1))
                    steps.did(v.tensor_tensor(s_inv, s_sum, s_exp, ALU.add))
                    steps.wait()
                    steps.did(v.reciprocal(s_inv, s_inv))
                    steps.wait()
                    v.tensor_tensor(Sc[:, b, :, lo_:], Sc[:, b, :, lo_:],
                                    s_inv.unsqueeze(2).to_broadcast([P, HG, 2 * P - lo_]), ALU.mult).then_inc(p_ready, 1)

                def glu_lo(u):
                    lo(g * 4 + (U_GLU + u + 1), u % 2)

                glu_lo(1)
                score(0)
                score(1)
                glu_lo(2)
                norm(0)
                norm(1)
                score(2)
                glu_lo(3)
                norm(2)
                score(3)
                glu_lo(4)
                norm(3)
                v.wait_ge(halves, g * 8 + 2 * (U_GLU + 4))
                for b in range(2):
                    v.wait_ge(free[b], g + (FREE["glu"][b] + 1))
                    v.tensor_tensor(uT[:, bass.ds(g * 2 + b, 1), PAD:].rearrange("p a t -> p (a t)"),
                                    PS[:, 2 + b, :], glusig[:, b, :], ALU.mult).then_inc(free[2 + b], 1)
                for b in range(2):
                    v.wait_ge(free[2 + b], g + (FREE["glu"][2 + b] + 1))
                    v.sem_inc(glu_done, 1)
                return steps.n

            per_block = glu_attn(0, True, 0)
            with v.Fori(1, TB) as g:
                glu_attn(g, False, g * per_block)

            def mix(branch, g, phase, ln):
                n0, s0 = U_MIX + 6 * MIX_IT * branch, S_MIX + 4 * MIX_IT * branch
                for u in (1, 2, 3):
                    lo(g * 4 + (s0 + u + 1), u % 2)
                    if branch == 0:
                        conv(g, 12 * (u - 1), 12 * u)
                    if ln and u == 1:
                        v.wait_ge(free[4], FREE["ln"][4] + 1)
                        for c in range(CC):
                            v.tensor_tensor(uT[:, c, 0:T], uT[:, c, 0:T], mu, ALU.subtract).then_inc(centred, 1)
                    if ln and u == 2:
                        v.wait_ge(sq_used, CC)
                        v.tensor_scalar(rstd, PS[:, 5, :], LN_EPS, None, ALU.add).then_inc(free[5], 1)
                    if ln and u == 3:
                        v.wait_ge(lnstd_done, 1)
                        steps = Steps(ln_step)
                        steps.did(v.reciprocal(rstd, rstd))
                        steps.wait()
                        for c in range(CC):
                            steps.did(v.tensor_tensor(uT[:, c, 0:T], uT[:, c, 0:T], rstd, ALU.mult))
                for j in range(4):
                    bank = 4 + j
                    if j % 2 == 0:
                        if branch == 0 and j == 0:
                            conv(g, 36, 50)
                        v.wait_ge(halves, g * 12 + 2 * (n0 + 5 + j // 2))
                    v.wait_ge(free[j], g + (FREE[phase][j] + 1))
                    v.tensor_tensor(sig[:, j, :], PS[:, bank, :], sig[:, j, :], ALU.mult).then_inc(free[bank], 1)
                    if j % 2:
                        for b in (j - 1, j):
                            v.wait_ge(free[4 + b], g + (FREE[phase][4 + b] + 1))
                            chunk = mixT[:, bass.ds(g * 4 + b, 1), :].rearrange("p a t -> p (a t)")
                            if branch == 0:
                                v.tensor_copy(chunk, sig[:, b, :]).then_inc(mix_ready, 1)
                            else:
                                v.tensor_tensor(chunk, chunk, sig[:, b, :], ALU.add).then_inc(mix_ready, 1)
                    if j == 1:
                        if branch == 0:
                            conv(g, 50, 2 * TAPS)
                        lo(g * 4 + (s0 + 5), 0)

            with v.Fori(0, MIX_IT) as g:
                mix(0, g, "mixA", False)
            mix(1, 0, "mixB", True)
            with v.Fori(1, MIX_IT) as g:
                mix(1, g, "mixB", False)
            for k in range(4):
                v.wait_ge(aT_hi, KD + k + 1)
                v.tensor_tensor(aTl[:, 4 * k:4 * k + 4, :], mixT[:, 4 * k:4 * k + 4, :],
                                aTh[:, 4 * k:4 * k + 4, :].bitcast(F32), ALU.subtract).then_inc(aT_lo, 1)

            with v.Fori(0, 4) as it:
                for u in range(4):
                    lo(it * 4 + (S_OUT + u + 2), (u + 1) % 2)
                    if u % 2:
                        v.wait_ge(x_reloaded, 16)
                        v.wait_ge(halves, it * 8 + 2 * (U_OUT + u + 1))
                        for m in range(TB):
                            bank = 4 * (u // 2) + m
                            h = XH[:, m, bass.ds(it * 2 * UC + (u // 2) * UC, UC)]
                            v.tensor_tensor(h, PS[:, bank, 0:UC], h, ALU.add).then_inc(free[bank], 1)

            for k in range(KD):
                v.wait_ge(aT_hi, KD + 4 + k + 1)
                v.scalar_tensor_tensor(out=aTl[:, k, :], in0=PS[:, k % 4, :], scalar=g2T[:, k:k + 1],
                                       in1=aTh[:, k, :].bitcast(F32), op0=ALU.mult, op1=ALU.subtract)\
                 .then_inc(free[k % 4], 1)
            v.wait_ge(squares_done, 2 * TB)
            mean_square(stat[:, 0:4], stat[:, 4:8]).then_inc(meansq_done, 1)
            v.wait_ge(std_done, 2)
            v.reciprocal(stat[:, 12:16], stat[:, 8:12]).then_inc(inv_done, 1)
            v.wait_ge(inv_done, 2)

            def rank(it, j, blocks=range(TB), base=None):
                bank = 4 + j
                i = it * 4 + j
                b0, b1 = blocks[0], blocks[-1] + 1
                steps = Steps(rank_step, it * (4 * RANK_STEPS) + RANK_STEPS * j if base is None else base)
                v.wait_ge(full[bank], it + (FULL["pq"][bank] + 1))
                v.nop(nofuse=True)

                def src(m):
                    return PS[:, bank, m * NK:(m + 1) * NK]

                for m in blocks:
                    steps.did(v.max(bestv[:, m, 0:8], src(m)))
                steps.wait()
                for m in blocks:
                    steps.did(v.max_index(besti[:, m, 0:8], bestv[:, m, 0:8], src(m)))
                for m in blocks:
                    steps.did(v.match_replace(sc[:, m, :], bestv[:, m, 0:8], src(m), MASKED))
                steps.wait()
                v.sem_inc(free[bank], 1)
                for m in blocks:
                    steps.did(v.max(bestv[:, m, 8:16], sc[:, m, :]))
                steps.wait()
                for m in blocks:
                    steps.did(v.max_index(besti[:, m, 8:16], bestv[:, m, 8:16], sc[:, m, :]))
                steps.wait()
                steps.did(v.tensor_tensor(topv[:, b0:b1, bass.ds(i, 1), :].rearrange("p m a k -> p m (a k)"), bestv[:, b0:b1, :],
                                          stat[:, 12 + b0:12 + b1].unsqueeze(2).to_broadcast([P, b1 - b0, TOPK]), ALU.mult))
                steps.did(v.tensor_copy(topi[:, b0:b1, bass.ds(i, 1), :].rearrange("p m a k -> p m (a k)"), besti[:, b0:b1, :]))
                steps.wait()
                return steps.base + steps.n

            def choose(m, h):
                steps = Steps(head_step, m * (PH * HEAD_STEPS) + h * HEAD_STEPS)
                one, two = bass.ds(m, 1), bass.ds(h * 2, 2)
                tv, ti = (t[:, one, two, :].rearrange("p a s k -> p (a s) k") for t in (topv, topi))
                steps.did(v.tensor_tensor(cand, tv[:, 0, :].unsqueeze(2).to_broadcast([P, TOPK, TOPK]),
                                          tv[:, 1, :].unsqueeze(1).to_broadcast([P, TOPK, TOPK]), ALU.add))
                steps.wait()
                sums = cand.rearrange("p a b -> p (a b)")
                steps.did(v.max(sumv[:, 0:8], sums))
                steps.wait()
                steps.did(v.max_index(sumi[:, 0:8], sumv[:, 0:8], sums))
                steps.did(v.match_replace(cand2, sumv[:, 0:8], sums, MASKED))
                steps.wait()
                steps.did(v.max(sumv[:, 8:16], cand2))
                steps.wait()
                steps.did(v.max_index(sumi[:, 8:16], sumv[:, 8:16], cand2))
                steps.did(v.tensor_copy(tops[:, bass.ds(h, 1), :].rearrange("p a k -> p (a k)"), sumv))
                steps.wait()
                steps.did(v.tensor_scalar(sump[:, 0, :], sumi, 4, None, ALU.logical_shift_right))
                steps.did(v.tensor_scalar(sump[:, 1, :], sumi, TOPK - 1, None, ALU.bitwise_and))
                steps.wait()
                steps.did(v.tensor_copy(sumf, sump))
                steps.wait()
                steps.did(v.tensor_tensor(pick, sumf.unsqueeze(3).to_broadcast([P, 2, TOPK, TOPK]),
                                          iota16[:, :].unsqueeze(1).unsqueeze(1).to_broadcast([P, 2, TOPK, TOPK]), ALU.is_equal))
                steps.wait()
                steps.did(v.tensor_tensor(pick, pick, ti.unsqueeze(2).to_broadcast([P, 2, TOPK, TOPK]), ALU.mult))
                steps.wait()
                steps.did(v.tensor_reduce(isel, pick, AX.X, ALU.add))
                steps.wait()
                steps.did(v.scalar_tensor_tensor(out=idx[:, one, bass.ds(h * TOPK, TOPK)].rearrange("p a k -> p (a k)"),
                                                 in0=isel[:, 0, :], scalar=float(NK), in1=isel[:, 1, :],
                                                 op0=ALU.mult, op1=ALU.add))
                steps.wait()
                v.sem_inc(idx_ready, 1)
                assert steps.n == HEAD_STEPS

            def gate_shift(m):
                steps = Steps(gate_step, m * 4)
                steps.did(v.tensor_copy(rs[:, 0, :], tops[:, :, 0]))
                steps.wait()
                v.tensor_tensor(tops, tops, rs[:, 0, :].unsqueeze(2).to_broadcast([P, PH, TOPK]),
                                ALU.subtract).then_inc(sub_ready, 1)

            def gate_norm(m):
                steps = Steps(gate_step, m * 4 + 1)
                v.wait_ge(gexp_done, m + 1)
                steps.did(v.tensor_reduce(rs[:, 0, :], tops, AX.X, ALU.add))
                steps.wait()
                steps.did(v.reciprocal(rs[:, 1, :], rs[:, 0, :]))
                steps.wait()
                steps.did(v.tensor_tensor(gates[:, :].rearrange("p (h k) -> p h k", h=PH), tops,
                                          rs[:, 1, :].unsqueeze(2).to_broadcast([P, PH, TOPK]), ALU.mult))
                steps.wait()

            def peer_q(it, first, last):
                for u in range(4):
                    if not (last and u == 3):
                        lo(it * 4 + (S_PQ + u + 2), (u + 1) % 2)
                    if not first:
                        if u == 0:
                            choose(0, it * 2 - 2)
                        if u == 1:
                            rank(it - 1, 2)
                            rank(it - 1, 3)
                        if u == 2:
                            choose(0, it * 2 - 1)
                    if u == 3:
                        rank(it, 0)
                        rank(it, 1)

            peer_q(0, True, False)
            with v.Fori(1, 3) as it:
                peer_q(it, False, False)
            peer_q(3, False, True)
            choose(0, PH - 2)
            ranked = RANK_STEPS * (4 * 4 - 2)
            for blocks in (range(1), range(1, TB)):
                for j in (2, 3):
                    ranked = rank(3, j, blocks, ranked)
                if blocks[0] == 0:
                    choose(0, PH - 1)

            def xn_to_psum(m):
                v.scalar_tensor_tensor(out=xn_ps, in0=XH[:, bass.ds(m, 1), :].rearrange("p a n -> p (a n)"),
                                       scalar=stat[:, bass.ds(m + 12, 1)], in1=g2b, op0=ALU.mult, op1=ALU.mult)\
                 .then_inc(xn_in_psum, 1)

            def add_v(m, r, tiles):
                for n in range(tiles):
                    s = n % RING
                    v.wait_ge(gathered[s], m * (32 * (HK // RING)) + r * (2 * tiles) + 16 * (HK // RING + 1 + n // RING))
                    v.wait_ge(tile_used, m * 2 * HK + r * tiles + (RING + HK + n))
                    v.scalar_tensor_tensor(out=y_ps, in0=ring[:, s, :], scalar=hact[:, bass.ds(r * tiles + n, 1)],
                                           in1=y_ps, op0=ALU.mult, op1=ALU.add).then_inc(tile_used, 1)

            def experts(m, last):
                v.wait_ge(xn_in_psum, m + 1)
                v.nop(nofuse=True)
                with v.Fori(0, HK // RING) as r:
                    for s in range(RING):
                        v.wait_ge(gathered[s], m * (32 * (HK // RING)) + r * 16 + 16)
                        v.scalar_tensor_tensor(out=ring[:, s, :], in0=ring[:, s, :], scalar=1.0, in1=xn_ps,
                                               op0=ALU.mult, op1=ALU.mult,
                                               accum_out=hid[:, bass.ds(r * RING + s, 1)]).then_inc(tile_used, 1)
                v.wait_ge(tile_used, m * 2 * HK + (RING + HK))
                v.memset(y_ps, 0.0).then_inc(y_cleared, 1)
                gate_norm(m)
                v.wait_ge(gelu_done, m + 1)
                v.tensor_tensor(hact[:, :], hact[:, :], gates[:, :], ALU.mult).then_inc(hact_ready, 1)
                if not last:
                    xn_to_psum(m + 1)
                v.wait_ge(y_cleared, m + 1)
                v.wait_ge(hact_ready, m + 1)
                v.nop(nofuse=True)
                with v.Fori(0, PH) as h:
                    if not last:
                        choose(m + 1, h)
                    add_v(m, h, HK // PH)
                if not last:
                    gate_shift(m + 1)
                v.wait_ge(tile_used, m * 2 * HK + (RING + 2 * HK))
                hm = XH[:, bass.ds(m, 1), :].rearrange("p a n -> p (a n)")
                v.tensor_tensor(hm, y_ps, hm, ALU.add).then_inc(y_added, 1)
                v.wait_ge(fin_sq, m + 1)
                mean_square(stat[:, 0:1], stat[:, 1:2]).then_inc(fin_ms, 1)
                v.wait_ge(fin_std, m + 1)
                v.reciprocal(stat[:, 3:4], stat[:, 2:3]).then_inc(fin_step, 1)
                v.wait_ge(fin_step, m + 1)
                v.scalar_tensor_tensor(out=hm, in0=hm, scalar=stat[:, 3:4], in1=gfin, op0=ALU.mult,
                                       op1=ALU.mult).then_inc(out_ready, 1)

            v.sem_inc(tile_used, RING)
            v.wait_ge(keys_loaded, 16 * 3)
            gate_shift(0)
            xn_to_psum(0)
            with v.Fori(0, TB - 1) as m:
                experts(m, False)
            experts(TB - 1, True)

    return nc


_INS = ["x", "norm_mix_g", "w_in", "conv_dw_w", "conv_dw_b", "conv_ln_g", "conv_ln_b", "w_conv_out", "attn_sinks",
        "w_attn_out", "w_out", "norm_ffn_g", "peer_w_q", "peer_sub_keys", "peer_u", "peer_v", "final_norm_g"]


def kernel(**inputs):
    import concourse.bacc as bacc
    from concourse.bass_utils import run_bass_kernel_spmd

    nc = bacc.Bacc("TRN2", target_bir_lowering=False, num_devices=1)
    arrays, args = {}, []
    for name in _INS:
        a = np.ascontiguousarray(inputs[name])
        arrays[f"in_{name}"] = a
        args.append(nc.dram_tensor(f"in_{name}", a.shape, mybir.dt.from_np(a.dtype), kind="ExternalInput").ap())
    shape = arrays["in_x"].shape
    args.append(nc.dram_tensor("out_h", shape, F32, kind="ExternalOutput").ap())
    build(nc, *args)
    r = run_bass_kernel_spmd(nc, [arrays], core_ids=[0])
    return r.results[0]["out_h"]
```

```python
from contextlib import ExitStack

import numpy as np

import concourse.bass as bass
from concourse import mybir

F32 = mybir.dt.float32
F32R = mybir.dt.float32r
U32 = mybir.dt.uint32
I32 = mybir.dt.int32
ALU = mybir.AluOpType
ACT = mybir.ActivationFunctionType
AX = mybir.AxisListType

P = 128
T = 512
TB = T // P
D = 2048
KD = D // P
CONV = 1024
CC = CONV // P
TAPS = 31
PAD = TAPS - 1
NQ, NKV, HD = 16, 2, 64
QDIM = NQ * HD
Q0 = 2 * CONV
K0 = Q0 + QDIM
V0 = K0 + NKV * HD
G0 = V0 + NKV * HD
CHUNK = 64
PH = 8
NK = 128
TOPK = 16
HK = PH * TOPK
RMS_EPS = 1e-6
LN_EPS = 1e-5
MASKED = -3.0e38
UK, UC = 8, 256
RING = 8
RANK_STEPS = 5 * TB + 2
HEAD_STEPS = 14
CONV_AT = (0, 12, 24, 36, 46, 54, 2 * TAPS)
HG = 4
SLOPES = [float(np.float32(np.power(np.float32(2.0), np.float32(-8.0 * (h + 1) / NQ)))) for h in range(NQ)]

U_Q = 0
U_KV = U_Q + 8
U_GLU = U_KV + 2
U_MIX = U_GLU + 16
MIX_IT = D // (2 * UC)
U_OUT = U_MIX + 2 * 6 * MIX_IT
U_PQ = U_OUT + 16

FREE, FULL = {}, {}


def _count_banks():
    free, full = [0] * 8, [0] * 8
    steps = [
        ("xT", [4, 4, 4, 4, 1, 0, 0, 0], [4, 4, 4, 4, 1, 0, 0, 0]),
        ("q", [2, 2, 2, 2, 0, 0, 0, 0], [0] * 8),
        ("kv", [1, 1, 0, 0, 0, 0, 0, 0], [0] * 8),
        ("kdup", [0, 0, 1, 1, 0, 0, 0, 0], [0, 0, 1, 1, 0, 0, 0, 0]),
        ("vtok", [1, 0, 0, 0, 0, 0, 0, 0], [1, 0, 0, 0, 0, 0, 0, 0]),
        ("glu", [4, 4, 4, 4, 0, 0, 0, 0], [0] * 8),
        ("attn", [0, 0, 0, 0, 16, 16, 32, 16], [0, 0, 0, 0, 16, 16, 32, 16]),
        ("mixA", [4] * 8, [0] * 8),
        ("ln", [0, 0, 0, 0, 1, 1, 0, 0], [0, 0, 0, 0, 1, 0, 0, 0]),
        ("mixB", [4] * 8, [0] * 8),
        ("out", [4] * 8, [0] * 8),
        ("xnT", [4, 4, 4, 4, 0, 0, 0, 0], [4, 4, 4, 4, 0, 0, 0, 0]),
        ("keys", [0, 0, 0, 0, 1, 1, 1, 1], [0, 0, 0, 0, 1, 1, 1, 1]),
        ("pq", [4] * 8, [0, 0, 0, 0, 4, 4, 4, 4]),
        ("end", [0] * 8, [0] * 8),
    ]
    for name, given_back, filled in steps:
        FREE[name], FULL[name] = list(free), list(full)
        free = [a + b for a, b in zip(free, given_back)]
        full = [a + b for a, b in zip(full, filled)]


_count_banks()


def build(nc, x, norm_mix_g, w_in, conv_dw_w, conv_dw_b, conv_ln_g, conv_ln_b, w_conv_out, attn_sinks,
          w_attn_out, w_out, norm_ffn_g, peer_w_q, peer_sub_keys, peer_u, peer_v, final_norm_g, out):
    ctx = ExitStack()
    with ctx:
        def sb(name, shape, dt=F32, stack=ctx):
            return stack.enter_context(nc.sbuf_tensor(name, shape, dt))

        def sem(name):
            return ctx.enter_context(nc.semaphore(name))

        ident = sb("ident", [P, P])
        lnmean = sb("lnmean", [P, P])
        negdist = sb("negdist", [P, 2 * P])
        disti = sb("disti", [P, 2 * P], I32)
        vecs = sb("vecs", [P, 56 + 8 * TAPS])
        sinks = sb("sinks", [P, NQ])
        stat = sb("stat", [P, 16])
        soft = sb("soft", [P, 2, 6, HG])
        iota16i = sb("iota16i", [P, TOPK], I32)
        iota16 = sb("iota16", [P, TOPK])
        again = ExitStack()
        XHr = sb("XHr", [P, TB, D], F32R, again)
        Br = sb("Br", [P, CC * (T + PAD) + QDIM // P * T], F32R, again)
        Gr = sb("Gr", [P, 6400], F32R, again)
        again.close()
        XH = sb("XH", [P, TB, D])
        B = sb("B", [P, CC * (T + PAD) + QDIM // P * T])
        G = sb("G", [P, 6400])
        g1T, g2T = vecs[:, 0:16], vecs[:, 40:56]
        cbT, lgT, lbT = vecs[:, 16:24], vecs[:, 24:32], vecs[:, 32:40]
        cwT = vecs[:, 56:56 + 8 * TAPS].rearrange("p (t c) -> p t c", c=CC)
        xhf = XH[:, :, :].rearrange("p m n -> p (m n)")
        mixT = xhf.rearrange("p (k t) -> p k t", t=T)
        qT = xhf[:, 0:4096].rearrange("p (c t) -> p c t", t=T)
        kT = xhf[:, 4096:5120].rearrange("p (g t) -> p g t", g=NKV)
        vtok = xhf[:, 5120:5632].rearrange("p (m d) -> p m d", d=P)
        Sc = xhf[:, 5632:7680].rearrange("p (b h s) -> p b h s", b=2, h=HG)
        uT = B[:, 0:CC * (T + PAD)].rearrange("p (c t) -> p c t", c=CC)
        OT = B[:, CC * (T + PAD):].rearrange("p (c t) -> p c t", t=T)
        g2b, gfin, squares = B[:, 0:D], B[:, D:2 * D], B[:, 2 * D:3 * D]
        idx = B[:, 6144:6656].bitcast(U32).rearrange("p (m k) -> p m k", m=TB)
        cand = B[:, 6656:6912].rearrange("p (a b) -> p a b", b=TOPK)
        cand2 = B[:, 6912:7168]
        pick = B[:, 7168:7680].rearrange("p (s a b) -> p s a b", s=2, b=TOPK)
        tops = B[:, 7680:7808].rearrange("p (h k) -> p h k", h=PH)
        sumv, sumi = B[:, 7808:7824], B[:, 7824:7840].bitcast(U32)
        sump = B[:, 7840:7872].bitcast(U32).rearrange("p (s k) -> p s k", s=2)
        sumf = B[:, 7872:7904].rearrange("p (s k) -> p s k", s=2)
        isel = B[:, 7904:7936].rearrange("p (s k) -> p s k", s=2)
        PT = G[:, 0:2048].rearrange("p (b h s t) -> p b h s t", b=2, h=HG, s=2)
        qblk = G[:, 2048:3072].rearrange("p (c t) -> p c t", t=P)
        vblk = G[:, 3072:3328].rearrange("p (s d) -> p s d", s=2)
        acc = G[:, 3328:4352].rearrange("p (b t) -> p b t", b=2)
        kblk = G[:, 3840:4352].rearrange("p (g t) -> p g t", g=NKV)
        mu = G[:, 4352:4864]
        rstd = G[:, 4864:5376]
        usum = rstd
        sq = G[:, 5376:6400].rearrange("p (b t) -> p b t", b=2)
        vrows = G[:, 5376:5760].rearrange("p (r n) -> p r n", n=P)
        kvT = G[:, 4352:5376].rearrange("p (b t) -> p b t", b=2)
        sig = G[:, 0:2048].rearrange("p (b t) -> p b t", t=T)
        glusig = sq
        OT_hi = [(0, Gr[:, 2048:3072].rearrange("p (c t) -> p c t", t=T)),
                 (2, Gr[:, 4352:6400].rearrange("p (c t) -> p c t", t=T)),
                 (6, XHr[:, TB - 1, D - 2 * T:].rearrange("p (c t) -> p c t", t=T))]
        OT_lo = uT_hi = Br[:, CC * (T + PAD):].rearrange("p (c t) -> p c t", t=T)
        uT_lo = Br[:, 0:CC * (T + PAD)].rearrange("p (c t) -> p c t", c=CC)
        skT = G[:, 0:2048].rearrange("p (i n) -> p i n", n=NK)
        skraw = G[:, 2048:4096].rearrange("p (i d) -> p i d", d=P)
        qchunk = G[:, 2048:3072].rearrange("p (b t) -> p b t", b=2)
        sc = G[:, 3072:3584].rearrange("p (m n) -> p m n", m=TB)
        topv = G[:, 4096:5120].rearrange("p (m i k) -> p m i k", m=TB, i=2 * PH)
        topi = G[:, 5120:6144].rearrange("p (m i k) -> p m i k", m=TB, i=2 * PH)
        bestv = G[:, 3584:3648].rearrange("p (m k) -> p m k", m=TB)
        besti = G[:, 3648:3712].bitcast(U32).rearrange("p (m k) -> p m k", m=TB)

        early = ExitStack()
        aTh = sb("aTh", [P, KD, T], F32R, early)
        aTl = sb("aTl", [P, KD, T], F32R, early)
        Wh = sb("Wh", [P, 2, UK, UC], F32R, early)
        Wl = sb("Wl", [P, 2, UK, UC], F32R, early)
        raw = sb("raw", [P, 2, UK, UC], F32, early)
        early.close()
        ring = sb("ring", [P, RING, D])
        rs = sb("rs", [P, 2, PH])
        gates = sb("gates", [P, HK])
        idxs = sb("idxs", [P, 2 * RING], U32)
        hid = sb("hid", [P, HK])
        hact = sb("hact", [P, HK])

        PS = ctx.enter_context(nc.psum_tensor("PS", [P, 8, T], F32))
        xn_ps = PS[:, 0:4, :].rearrange("p b t -> p (b t)")
        y_ps = PS[:, 4:8, :].rearrange("p b t -> p (b t)")

        w_loaded = [sem("w_loaded0"), sem("w_loaded1")]
        hi_done, lo_done = sem("hi_done"), sem("lo_done")
        halves = sem("halves")
        full = [sem(f"bank_full{b}") for b in range(8)]
        free = [sem(f"bank_free{b}") for b in range(8)]
        x_loaded = [sem(f"x_loaded{m}") for m in range(TB)]
        consts_loaded, keys_loaded, x_reloaded = (sem(n) for n in ("consts_loaded", "keys_loaded", "x_reloaded"))
        pool_const, dve_const = sem("pool_const"), sem("dve_const")
        squares_done, meansq_done, std_done, inv_done, norm_done = (
            sem(n) for n in ("squares_done", "meansq_done", "std_done", "inv_done", "norm_done"))
        aT_hi, aT_lo = sem("aT_hi"), sem("aT_lo")
        glu_done, conv_step = sem("glu_done"), sem("conv_step")
        sum_step, centred, squared, sq_used, lnstd_done, ln_step = (
            sem(n) for n in ("sum_step", "centred", "squared", "sq_used", "lnstd_done", "ln_step"))
        silu_done, out_hi, out_lo = sem("silu_done"), sem("out_hi"), sem("out_lo")
        blk_staged = sem("blk_staged")
        attn_step, negmax_ready, exp_done, p_ready = (
            sem(n) for n in ("attn_step", "negmax_ready", "exp_done", "p_ready"))
        mix_ready = sem("mix_ready")
        rank_step, head_step, gate_step, sub_ready, gexp_done, idx_ready = (
            sem(n) for n in ("rank_step", "head_step", "gate_step", "sub_ready", "gexp_done", "idx_ready"))
        staged = sem("staged")
        gathered = [sem(f"gathered{s}") for s in range(RING)]
        tile_used = sem("tile_used")
        y_cleared = sem("y_cleared")
        xn_in_psum, gelu_done, hact_ready = sem("xn_in_psum"), sem("gelu_done"), sem("hact_ready")
        y_added, fin_sq, fin_ms, fin_std, fin_step, out_ready, stored = (
            sem(n) for n in ("y_added", "fin_sq", "fin_ms", "fin_std", "fin_step", "out_ready", "stored"))

        block = ctx.enter_context(nc.Block())

        @block.sync
        def _(sp):
            xt = x[0].rearrange("(m p) n -> p m n", p=P)
            for m in range(TB):
                sp.dma_start(XH[:, m, :], xt[:, m, :]).then_inc(x_loaded[m], 16)
            rows = [norm_mix_g[0].rearrange("(k p) -> k p", p=P), conv_dw_b[0].rearrange("(k p) -> k p", p=P),
                    conv_ln_g[0].rearrange("(k p) -> k p", p=P), conv_ln_b[0].rearrange("(k p) -> k p", p=P),
                    norm_ffn_g[0].rearrange("(k p) -> k p", p=P)]
            at = 0
            for r in rows:
                sp.dma_start(vrows[at:at + r.shape[0], 0, :], r).then_inc(consts_loaded, 16)
                at += r.shape[0]
            cw = conv_dw_w[0].rearrange("t (c p) -> (t c) p", p=P)
            half = 4 * TAPS
            for j in range(2):
                sp.dma_start(vrows[0:half, 1 + j, :], cw[j * half:(j + 1) * half, :]).then_inc(consts_loaded, 16)
            sp.dma_start(sinks[:, :], attn_sinks[0:1, :].to_broadcast([P, NQ])).then_inc(consts_loaded, 16)

            def load(src, k0, c0, slot):
                sp.nop(nofuse=True)
                view = src[k0 * P:(k0 + UK) * P, :].rearrange("(k p) n -> p k n", p=P)
                sp.dma_start(raw[:, slot, :, :], view[:, :, bass.ds(c0, UC)]).then_inc(w_loaded[slot], 16)

            def q_units(it):
                for u in range(4):
                    if it or u >= 2:
                        sp.wait_ge(lo_done, 4 * it + u - 1)
                    load(w_in[0], (u % 2) * UK, it * 2 * UC + Q0 + u // 2 * UC, u % 2)

            q_units(0)
            q_units(1)
            for u in range(2):
                sp.wait_ge(lo_done, U_KV + u - 1)
                load(w_in[0], u * UK, K0, u)
            with sp.Fori(0, 4) as g:
                for u in range(4):
                    sp.wait_ge(lo_done, g * 4 + (U_GLU + u - 1))
                    load(w_in[0], (u % 2) * UK, g * UC + (CONV if u < 2 else 0), u % 2)

            for branch, gate0, w_branch in ((0, G0 + D, w_attn_out), (1, G0, w_conv_out)):
                with sp.Fori(0, MIX_IT) as g:
                    n0 = U_MIX + 6 * MIX_IT * branch
                    for u in range(6):
                        sp.wait_ge(lo_done, g * 6 + (n0 + u - 1))
                        if u < 4:
                            load(w_in[0], (u % 2) * UK, g * 2 * UC + (gate0 + u // 2 * UC), u % 2)
                        else:
                            load(w_branch[0], 0, g * 2 * UC + (u % 2) * UC, u % 2)

            def out_units(it):
                for u in range(4):
                    sp.wait_ge(lo_done, it * 4 + (U_OUT + u - 1))
                    load(w_out[0], (u % 2) * UK, it * 2 * UC + (u // 2) * UC, u % 2)

            out_units(0)
            sp.wait_ge(halves, 2 * U_OUT)
            sp.dma_start(g2b, norm_ffn_g[0:1, :].to_broadcast([P, D])).then_inc(keys_loaded, 16)
            sp.dma_start(gfin, final_norm_g.rearrange("(a n) -> a n", a=1).to_broadcast([P, D])).then_inc(keys_loaded, 16)
            with sp.Fori(1, 4) as it:
                out_units(it)
            sp.dma_start(skraw, peer_sub_keys[0].rearrange("h s n d -> n (h s) d")).then_inc(keys_loaded, 16)
            with sp.Fori(0, 4) as it:
                for u in range(4):
                    sp.wait_ge(lo_done, it * 4 + (U_PQ + u - 1))
                    load(peer_w_q[0], (u % 2) * UK, it * 2 * UC + (u // 2) * UC, u % 2)
            ot = out[0].rearrange("(m p) n -> p m n", p=P)
            with sp.Fori(0, TB) as m:
                sp.wait_ge(out_ready, m + 1)
                sp.dma_start(ot[:, bass.ds(m, 1), :], XH[:, bass.ds(m, 1), :]).then_inc(stored, 16)
            sp.wait_ge(stored, 16 * TB)

        @block.gpsimd
        def _(pool):
            pool.memset(ident[:, :], 0.0).then_inc(pool_const, 1)
            pool.wait_ge(pool_const, 1)
            pool.affine_select(out=ident[:, :], in_=ident[:, :], compare_op=ALU.not_equal, fill=1.0,
                               base=0, pattern=[[-1, P]], channel_multiplier=1).then_inc(pool_const, 1)
            pool.iota(disti[:, :], pattern=[[-1, 2 * P]], base=P, channel_multiplier=1).then_inc(pool_const, 1)
            pool.iota(iota16i[:, :], pattern=[[1, TOPK]], base=0, channel_multiplier=0).then_inc(pool_const, 1)

            def stage(m, first):
                if first:
                    for b in range(4):
                        pool.wait_ge(free[b], FREE["glu"][b])
                    pool.tensor_copy(qblk, qT[:, :, 0:P]).then_inc(blk_staged, 1)
                    pool.tensor_copy(kblk[:, :, P:], kT[:, :, 0:P]).then_inc(blk_staged, 1)
                    pool.tensor_copy(vblk[:, 1, :], vtok[:, 0, :]).then_inc(blk_staged, 1)
                else:
                    pool.wait_ge(full[5], m * 4 + FULL["attn"][5])
                    pool.wait_ge(full[6], m * 8 + FULL["attn"][6])
                    pool.tensor_copy(qblk, qT[:, :, bass.ds(m * P, P)]).then_inc(blk_staged, 1)
                    pool.tensor_copy(kblk, kT[:, :, bass.ds((m - 1) * P, 2 * P)]).then_inc(blk_staged, 1)
                    pool.tensor_copy(vblk, vtok[:, bass.ds(m - 1, 2), :]).then_inc(blk_staged, 1)

            stage(0, True)
            with pool.Fori(1, TB) as m:
                stage(m, False)

            rounds = HK // (2 * RING)
            with pool.Fori(0, TB) as m:
                pool.wait_ge(idx_ready, m * PH + PH)
                pool.nop(nofuse=True)
                for part, table in enumerate((peer_u, peer_v)):
                    with pool.Fori(0, rounds) as r:
                        for h in range(2):
                            pool.tensor_copy(idxs[:, h * RING:(h + 1) * RING],
                                             idx[:, bass.ds(m, 1), bass.ds(r * 2 * RING + h * RING, RING)]
                                             .rearrange("p a k -> p (a k)")).then_inc(staged, 1)
                            pool.wait_ge(staged, m * (4 * rounds) + r * 2 + (part * 2 * rounds + h + 1))
                            for s in range(RING):
                                pool.wait_ge(tile_used, m * 2 * HK + r * 2 * RING + (part * HK + h * RING + s + 1))
                                pool.nop(nofuse=True)
                                pool.indirect_dma_start(
                                    ring[:, s, :], None, table[0],
                                    bass.IndirectOffsetOnAxis(idxs[:, h * RING + s:h * RING + s + 1], 0),
                                ).then_inc(gathered[s], 16)

        @block.scalar
        def _(act):
            for m in range(TB):
                act.wait_ge(x_loaded[m], 16)
                act.activation(aTl[:, 4 * m:4 * m + 4, :].rearrange("p k t -> p (k t)"), XH[:, m, :], ACT.Square,
                               accum_out=stat[:, m:m + 1]).then_inc(squares_done, 1)
            act.wait_ge(meansq_done, 1)
            act.activation(stat[:, 8:12], stat[:, 4:8], ACT.Sqrt).then_inc(std_done, 1)
            act.wait_ge(w_loaded[0], 16)
            act.activation(Wh[:, 0, :, :], raw[:, 0, :, :], ACT.Copy).then_inc(hi_done, 1)
            act.wait_ge(inv_done, 1)
            act.activation(XH[:, 3, :], XH[:, 3, :], ACT.Copy, scale=stat[:, 15:16]).then_inc(norm_done, 1)
            act.wait_ge(full[4], 1)
            act.activation(vecs[:, :], PS[:, 4, 0:56 + 8 * TAPS], ACT.Copy).then_inc(free[4], 1)
            act.wait_ge(free[4], 1)
            for k in range(KD):
                act.wait_ge(full[k % 4], k // 4 + 1)
                act.activation(aTh[:, k, :], PS[:, k % 4, :], ACT.Copy, scale=g1T[:, k:k + 1]).then_inc(aT_hi, 1)

            def hi(n, slot, loads, first=False):
                act.wait_ge(w_loaded[slot], loads)
                if not first:
                    act.wait_ge(halves, n * 2 - 2)
                act.activation(Wh[:, slot, :, :], raw[:, slot, :, :], ACT.Copy).then_inc(hi_done, 1)

            def hi4(it, base, u):
                hi(it * 4 + (base + u), u % 2, it * 32 + 16 * ((base + u) // 2 + 1))

            for it in range(2):
                for u in range(4):
                    n = it * 4 + u + 1
                    hi(n, n % 2, 16 * (n // 2 + 1), n < 2)
                    if u % 2:
                        act.wait_ge(halves, 2 * n)
                        for b in range(2):
                            act.activation(qT[:, it * 4 + u // 2 * 2 + b, :], PS[:, u // 2 * 2 + b, :], ACT.Copy,
                                           scale=HD ** -0.5).then_inc(free[u // 2 * 2 + b], 1)
            hi4(0, U_KV, 1)
            hi4(0, U_KV, 2)
            act.wait_ge(halves, 2 * U_GLU)
            for b in range(2):
                act.activation(kvT[:, b, :], PS[:, b, :], ACT.Copy).then_inc(free[b], 1)
            for b in (2, 3):
                act.wait_ge(full[b], FULL["kdup"][b] + 1)
                act.activation(kT[:, b - 2, :], PS[:, b, :], ACT.Copy).then_inc(free[b], 1)
            act.wait_ge(full[0], FULL["vtok"][0] + 1)
            act.activation(vtok, PS[:, 0, :].rearrange("p (m d) -> p m d", m=TB), ACT.Copy).then_inc(free[0], 1)

            def glu_attn(g, first):
                lo = P if first else 0

                def exps(hg):
                    b = hg % 2
                    act.wait_ge(negmax_ready, g * 4 + (hg + 1))
                    for i in range(HG):
                        act.activation(Sc[:, b, i, lo:], Sc[:, b, i, lo:], ACT.Exp, bias=soft[:, b, 1, i:i + 1],
                                       accum_out=soft[:, b, 2, i:i + 1])
                    act.activation(soft[:, b, 4, :], soft[:, b, 3, :], ACT.Exp).then_inc(exp_done, 1)

                def pt_copy(hg):
                    if not (first and hg < 2):
                        act.wait_ge(full[6], g * 8 + (FULL["attn"][6] + 2 * hg - 2))
                    for j in range(2):
                        act.wait_ge(full[6 + j], g * (8 - 4 * j) + (FULL["attn"][6 + j] + (2 - j) * hg + 1))
                        act.activation(PT[:, hg % 2, 2 * j:2 * j + 2, lo // P:, :],
                                       PS[:, 6 + j, :].rearrange("p (h s t) -> p h s t", h=2, s=2)[:, :, lo // P:, :],
                                       ACT.Copy).then_inc(free[6 + j], 1)

                def o_copy(hg):
                    act.wait_ge(full[6], g * 8 + (FULL["attn"][6] + 2 * hg + 2))
                    act.activation(OT[:, 2 * hg:2 * hg + 2, bass.ds(g * P, P)],
                                   PS[:, 6, 0:2 * P].rearrange("p (c t) -> p c t", c=2), ACT.Copy).then_inc(free[6], 1)

                hi4(g, U_GLU, 1)
                hi4(g, U_GLU, 2)
                exps(0)
                exps(1)
                hi4(g, U_GLU, 3)
                pt_copy(0)
                o_copy(0)
                if not first:
                    act.wait_ge(glu_done, g * 2)
                for b in range(2):
                    act.activation(glusig[:, b, :], PS[:, b, :], ACT.Sigmoid).then_inc(free[b], 1)
                exps(2)
                hi4(g, U_GLU, 4)
                pt_copy(1)
                o_copy(1)
                exps(3)
                pt_copy(2)
                o_copy(2)
                pt_copy(3)
                o_copy(3)

            glu_attn(0, True)
            with act.Fori(1, 4) as g:
                glu_attn(g, False)

            act.wait_ge(glu_done, CC)
            act.wait_ge(free[6], FREE["mixA"][6])
            for k0, view in OT_hi:
                act.activation(view, OT[:, k0:k0 + view.shape[1], :], ACT.Copy).then_inc(out_hi, 1)

            def mix_to_aT(k):
                act.activation(aTh[:, 4 * k:4 * k + 4, :], mixT[:, 4 * k:4 * k + 4, :], ACT.Copy).then_inc(aT_hi, 1)

            def mix(branch, g, ln, last):
                n0 = U_MIX + 6 * MIX_IT * branch

                def mix_hi(u):
                    hi(g * 6 + (n0 + u), u % 2, g * 48 + 16 * ((n0 + u) // 2 + 1))

                def sigmoids(first_bank, u):
                    act.wait_ge(halves, g * 12 + 2 * (n0 + u + 1))
                    for b in (first_bank, first_bank + 1):
                        act.activation(sig[:, b, :], PS[:, b, :], ACT.Sigmoid).then_inc(free[b], 1)

                mix_hi(1)
                mix_hi(2)
                if ln:
                    act.wait_ge(full[4], FULL["ln"][4] + 1)
                    act.activation(mu, PS[:, 4, :], ACT.Copy).then_inc(free[4], 1)
                    for c in range(CC):
                        act.wait_ge(centred, c + 1)
                        if c >= 2:
                            act.wait_ge(sq_used, c - 1)
                        act.activation(sq[:, c % 2, :], uT[:, c, 0:T], ACT.Square).then_inc(squared, 1)
                act.wait_ge(mix_ready, g * 4 + (4 * MIX_IT * branch + 1))
                sigmoids(0, 1)
                mix_hi(3)
                if ln:
                    act.wait_ge(free[5], FREE["ln"][5] + 1)
                    act.activation(rstd, rstd, ACT.Sqrt).then_inc(lnstd_done, 1)
                mix_hi(4)
                if ln:
                    for c in range(CC + 1):
                        if c < CC:
                            act.wait_ge(ln_step, 2 + c)
                            act.activation(uT[:, c, 0:T], uT[:, c, 0:T], ACT.Silu, bias=lbT[:, c:c + 1],
                                           scale=lgT[:, c:c + 1]).then_inc(silu_done, 1)
                        if c:
                            act.wait_ge(silu_done, c)
                            act.activation(uT_hi[:, c - 1, :], uT[:, c - 1, 0:T], ACT.Copy).then_inc(out_hi, 1)
                sigmoids(2, 3)
                mix_hi(5)
                if last:
                    act.wait_ge(mix_ready, 8 * MIX_IT - 3)
                    for k in range(3):
                        mix_to_aT(k)
                mix_hi(6)

            with act.Fori(0, MIX_IT) as g:
                mix(0, g, False, False)
            mix(1, 0, True, False)
            with act.Fori(1, MIX_IT - 1) as g:
                mix(1, g, False, False)
            mix(1, MIX_IT - 1, False, True)

            act.wait_ge(mix_ready, 8 * MIX_IT + 1)
            mix_to_aT(3)
            act.wait_ge(aT_lo, 4)
            act.dma_start(XH[:, :, :], x[0].rearrange("(m p) n -> p m n", p=P)).then_inc(x_reloaded, 16)
            with act.Fori(0, 4) as it:
                for u in range(4):
                    hi4(it, U_OUT, u + 1)

            for k in range(KD):
                act.wait_ge(full[k % 4], FULL["xnT"][k % 4] + k // 4 + 1)
                act.activation(aTh[:, k, :], PS[:, k % 4, :], ACT.Copy, scale=g2T[:, k:k + 1]).then_inc(aT_hi, 1)
            hi4(0, U_PQ, 1)
            for b in range(4, 8):
                act.wait_ge(full[b], FULL["keys"][b] + 1)
                act.activation(skT[:, 4 * b - 16:4 * b - 12, :], PS[:, b, :].rearrange("p (i n) -> p i n", i=4),
                               ACT.Copy).then_inc(free[b], 1)
            for m in range(TB):
                act.wait_ge(squares_done, TB + m)
                act.activation(squares, XH[:, m, :], ACT.Square, accum_out=stat[:, m:m + 1]).then_inc(squares_done, 1)
            act.wait_ge(meansq_done, 2)
            act.activation(stat[:, 8:12], stat[:, 4:8], ACT.Sqrt).then_inc(std_done, 1)

            def peer_q(it, first, last):
                for u in range(4):
                    if not (first and u == 0 or last and u == 3):
                        hi4(it, U_PQ, u + 1)
                    if u % 2:
                        act.wait_ge(halves, it * 8 + 2 * (U_PQ + u + 1))
                        for b in range(2):
                            last_bank = 6 + b if u == 1 else 4 + b
                            act.wait_ge(full[last_bank], it + (FULL["pq"][last_bank] + u // 2))
                            act.activation(qchunk[:, b, :], PS[:, u // 2 * 2 + b, :], ACT.Copy)\
                               .then_inc(free[u // 2 * 2 + b], 1)

            peer_q(0, True, False)
            with act.Fori(1, 3) as it:
                peer_q(it, False, False)
            peer_q(3, False, True)

            def gate_exp(m):
                act.wait_ge(sub_ready, m + 1)
                act.activation(tops, tops, ACT.Exp).then_inc(gexp_done, 1)

            def experts(m, last):
                act.wait_ge(y_cleared, m + 1)
                act.activation(hact[:, :], hid[:, :], ACT.Gelu_apprx_tanh).then_inc(gelu_done, 1)
                if not last:
                    gate_exp(m + 1)
                act.wait_ge(y_added, m + 1)
                act.activation(squares, XH[:, bass.ds(m, 1), :].rearrange("p a n -> p (a n)"), ACT.Square,
                               accum_out=stat[:, 0:1]).then_inc(fin_sq, 1)
                act.wait_ge(fin_ms, m + 1)
                act.activation(stat[:, 2:3], stat[:, 1:2], ACT.Sqrt).then_inc(fin_std, 1)

            gate_exp(0)
            with act.Fori(0, TB - 1) as m:
                experts(m, False)
            experts(TB - 1, True)

        @block.tensor
        def _(pe):
            pe.wait_ge(pool_const, 4)
            pe.wait_ge(consts_loaded, 16 * 8)
            half = 4 * TAPS
            pe.transpose(PS[:, 4, 0:56], vrows[0:56, 0, :], ident[0:56, 0:56])
            for j in range(2):
                ins = pe.transpose(PS[:, 4, 56 + j * half:56 + (j + 1) * half], vrows[0:half, 1 + j, :], ident[0:half, 0:half])
            ins.then_inc(full[4], 1)

            def to_xT(src, phase):
                for k in range(KD):
                    if FREE[phase][k % 4] + k // 4:
                        pe.wait_ge(free[k % 4], FREE[phase][k % 4] + k // 4)
                    for m in range(TB):
                        ins = pe.transpose(PS[:, k % 4, m * P:(m + 1) * P], src[:, m, k * P:(k + 1) * P], ident[:, :])
                    ins.then_inc(full[k % 4], 1)

            pe.wait_ge(norm_done, TB)
            to_xT(XH, "xT")

            def unit(n, slot, bank, start, stop, k0, acts=None, parts_before=None):
                pe.wait_ge(lo_done, n)
                hi, lo = acts or ([a[:, k0 + k, :] for k in range(UK)] for a in (aTh, aTl))
                for b in range(2):
                    for k in range(UK):
                        if parts_before is not None and b == 0:
                            pe.wait_ge(out_lo, parts_before + k + 1)
                        for j, (w, a) in enumerate(((Wh, hi[k]), (Wl, hi[k]), (Wh, lo[k]))):
                            ins = pe.matmul(PS[:, bank + b, :], w[:, slot, k, b * P:(b + 1) * P], a,
                                            start=start and k == 0 and j == 0, stop=stop and k == UK - 1 and j == 2)
                    ins.then_inc(halves, 1)

            def group(n, bank, it, phase):
                for b in range(2):
                    pe.wait_ge(free[bank + b], it + FREE[phase][bank + b])
                unit(n, 0, bank, True, False, 0)
                unit(n + 1, 1, bank, False, True, UK)

            for it in range(2):
                group(it * 4 + 1, 0, it, "q")
                group(it * 4 + 3, 2, it, "q")
            group(U_KV + 1, 0, 0, "kv")
            pe.wait_ge(free[0], FREE["kv"][0] + 1)
            for g in range(NKV):
                pe.wait_ge(free[2 + g], FREE["kdup"][2 + g])
                for b in range(2):
                    ins = pe.matmul(PS[b * HD:(b + 1) * HD, 2 + g, :], ident[:, g * HD:(g + 1) * HD], kvT[:, 0, :],
                                    start=True, stop=True)
                ins.then_inc(full[2 + g], 1)
            pe.wait_ge(free[1], FREE["kv"][1] + 1)
            for m in range(TB):
                ins = pe.transpose(PS[:, 0, m * P:(m + 1) * P], kvT[:, 1, m * P:(m + 1) * P], ident[:, :])
            ins.then_inc(full[0], 1)

            def glu_attn(g, first):
                parts = (1,) if first else (0, 1)

                def qk(hg):
                    for i in range(HG):
                        h, bank = HG * hg + i, 4 + i % 2
                        o = (h % 2) * HD
                        if i < 2:
                            pe.wait_ge(free[bank], g * 4 + (FREE["attn"][bank] + hg))
                        at, lo = (i // 2) * 2 * P, P if first else 0
                        ins = pe.matmul(PS[:, bank, at + lo:at + 2 * P], qblk[o:o + HD, h // 2, :],
                                        kblk[o:o + HD, h // PH, lo:], start=True, stop=True)
                        if i >= 2:
                            ins.then_inc(full[bank], 1)

                def transposes(hg):
                    pe.wait_ge(p_ready, g * 4 + (hg + 1))
                    for i in range(HG):
                        bank = 6 + i // 2
                        if i % 2 == 0 and not (first and hg == 0):
                            pe.wait_ge(free[bank], g * (8 if bank == 6 else 4) + (FREE["attn"][bank] + (2 if bank == 6 else 1) * hg))
                        for s in parts:
                            at = (i % 2) * 2 * P + s * P
                            ins = pe.transpose(PS[:, bank, at:at + P], Sc[:, hg % 2, i, s * P:(s + 1) * P], ident[:, :])
                        if i % 2:
                            ins.then_inc(full[bank], 1)

                def pv(hg):
                    pe.wait_ge(free[6], g * 8 + (FREE["attn"][6] + 2 * hg + 1))
                    pe.wait_ge(free[7], g * 4 + (FREE["attn"][7] + hg + 1))
                    for i in range(HG):
                        h = HG * hg + i
                        o = (h % 2) * HD
                        for s in parts:
                            ins = pe.matmul(PS[o:o + HD, 6, i // 2 * P:(i // 2 + 1) * P],
                                            vblk[:, s, h // PH * HD:(h // PH + 1) * HD], PT[:, hg % 2, i, s, :],
                                            start=s == parts[0], stop=s == 1)
                    ins.then_inc(full[6], 1)

                for b in range(2):
                    pe.wait_ge(free[b], g + FREE["glu"][b])
                unit(g * 4 + (U_GLU + 1), 0, 0, True, False, 0)
                pe.wait_ge(blk_staged, g * 3 + 3)
                qk(0)
                qk(1)
                unit(g * 4 + (U_GLU + 2), 1, 0, False, True, UK)
                transposes(0)
                qk(2)
                pv(0)
                for b in (2, 3):
                    pe.wait_ge(free[b], g + FREE["glu"][b])
                unit(g * 4 + (U_GLU + 3), 0, 2, True, False, 0)
                transposes(1)
                qk(3)
                pv(1)
                unit(g * 4 + (U_GLU + 4), 1, 2, False, True, UK)
                for hg in (2, 3):
                    transposes(hg)
                    pv(hg)

            glu_attn(0, True)
            with pe.Fori(1, 4) as g:
                glu_attn(g, False)

            def mix(branch, g, phase, ln):
                n0 = U_MIX + 6 * MIX_IT * branch
                for b in range(2):
                    pe.wait_ge(free[b], g + FREE[phase][b])
                unit(g * 6 + (n0 + 1), 0, 0, True, False, 0)
                if ln:
                    pe.wait_ge(sum_step, CC - 1)
                    pe.wait_ge(free[4], FREE["ln"][4])
                    pe.wait_ge(free[5], FREE["ln"][5])
                    pe.matmul(PS[:, 4, :], lnmean[:, :], usum, start=True, stop=True).then_inc(full[4], 1)
                unit(g * 6 + (n0 + 2), 1, 0, False, True, UK)
                if ln:
                    for c in range(CC):
                        pe.wait_ge(squared, c + 1)
                        pe.matmul(PS[:, 5, :], lnmean[:, :], sq[:, c % 2, :], start=c == 0, stop=c == CC - 1)\
                          .then_inc(sq_used, 1)
                group(g * 6 + (n0 + 3), 2, g, phase)
                if branch:
                    hi, lo = ([a[:, k, 0:T] for k in range(CC)] for a in (uT_hi, uT_lo))
                    if not ln:
                        pe.wait_ge(out_lo, len(OT_hi) + CC)
                else:
                    hi = [view[:, k, :] for _, view in OT_hi for k in range(view.shape[1])]
                    lo = [OT_lo[:, k, :] for k in range(CC)]
                    pe.wait_ge(out_lo, len(OT_hi))
                for slot in range(2):
                    bank = 4 + 2 * slot
                    for b in (bank, bank + 1):
                        pe.wait_ge(free[b], g + FREE[phase][b])
                    unit(g * 6 + (n0 + 5 + slot), slot, bank, True, True, 0, (hi, lo),
                         len(OT_hi) if ln and slot == 0 else None)

            pe.wait_ge(free[6], FREE["mixA"][6])
            with pe.Fori(0, MIX_IT) as g:
                mix(0, g, "mixA", False)
            mix(1, 0, "mixB", True)
            with pe.Fori(1, MIX_IT) as g:
                mix(1, g, "mixB", False)

            with pe.Fori(0, 4) as it:
                for u in range(4):
                    pe.wait_ge(lo_done, it * 4 + (U_OUT + u + 1))
                    pe.wait_ge(aT_lo, 2 + 2 * (u % 2))
                    for m in range(TB):
                        bank = 4 * (u // 2) + m
                        if u % 2 == 0:
                            pe.wait_ge(free[bank], it + FREE["out"][bank])
                        for k in range(UK):
                            for j, (a, w) in enumerate(((aTh, Wh), (aTl, Wh), (aTh, Wl))):
                                ins = pe.matmul(PS[:, bank, 0:UC], a[:, (u % 2) * UK + k, m * P:(m + 1) * P],
                                                w[:, u % 2, k, :], start=u % 2 == 0 and k == 0 and j == 0,
                                                stop=u % 2 == 1 and k == UK - 1 and j == 2)
                        if m % 2:
                            ins.then_inc(halves, 1)

            for b in range(8):
                pe.wait_ge(free[b], FREE["xnT"][b])
            to_xT(XH, "xnT")
            pe.wait_ge(keys_loaded, 16 * 3)
            for b in range(4, 8):
                for i in range(4):
                    ins = pe.transpose(PS[:, b, i * P:(i + 1) * P], skraw[:, 4 * (b - 4) + i, :], ident[:, :])
                ins.then_inc(full[b], 1)

            def scores(it, gg):
                for b in range(2):
                    bank = 4 + 2 * gg + b
                    pe.wait_ge(free[bank], it + FREE["pq"][bank])
                    pe.wait_ge(free[2 * gg + b], it + (FREE["pq"][2 * gg + b] + 1))
                    for m in range(TB):
                        ins = pe.matmul(PS[:, bank, m * P:(m + 1) * P], qchunk[:, b, m * P:(m + 1) * P],
                                        skT[:, bass.ds(it * 4 + (2 * gg + b), 1), :].rearrange("p a n -> p (a n)"),
                                        start=True, stop=True)
                    ins.then_inc(full[bank], 1)

            def peer_q(it, first):
                for b in (0, 1):
                    pe.wait_ge(free[b], it + FREE["pq"][b])
                unit(it * 4 + (U_PQ + 1), 0, 0, True, False, 0)
                if not first:
                    scores(it - 1, 1)
                unit(it * 4 + (U_PQ + 2), 1, 0, False, True, UK)
                for b in (2, 3):
                    pe.wait_ge(free[b], it + FREE["pq"][b])
                unit(it * 4 + (U_PQ + 3), 0, 2, True, False, 0)
                scores(it, 0)
                unit(it * 4 + (U_PQ + 4), 1, 2, False, True, UK)

            peer_q(0, True)
            with pe.Fori(1, 4) as it:
                peer_q(it, False)
            scores(3, 1)

        @block.vector
        def _(v):
            class Steps:

                def __init__(self, s, base=0):
                    self.s, self.base, self.n = s, base, 0

                def did(self, ins):
                    ins.then_inc(self.s, 1)
                    self.n += 1

                def wait(self):
                    v.wait_ge(self.s, self.base + self.n)
                    v.nop(nofuse=True)

            consts = Steps(dve_const)
            consts.did(v.memset(lnmean[:, :], 1.0 / CONV))
            v.wait_ge(pool_const, 4)
            consts.did(v.tensor_copy(iota16[:, :], iota16i[:, :]))
            consts.did(v.tensor_copy(negdist[:, :], disti[:, :]))
            consts.wait()
            consts.did(v.scalar_tensor_tensor(out=negdist[:, :], in0=negdist[:, :], scalar=-1.0, in1=negdist[:, :],
                                              op0=ALU.mult, op1=ALU.min))
            consts.wait()
            consts.did(v.memset(negdist[0:CHUNK, 0:CHUNK], MASKED))
            consts.did(v.memset(negdist[0:CHUNK, 3 * CHUNK:], MASKED))
            consts.did(v.memset(negdist[CHUNK:, 0:2 * CHUNK], MASKED))
            v.sem_inc(mix_ready, 1)

            def mean_square(squares, out_):
                return v.tensor_scalar(out_, squares, 1.0 / D, RMS_EPS, ALU.mult, ALU.add)

            def lo(n, slot):
                v.wait_ge(hi_done, n)
                v.tensor_tensor(Wl[:, slot, :, :], raw[:, slot, :, :], Wh[:, slot, :, :].bitcast(F32), ALU.subtract)\
                 .then_inc(lo_done, 1)

            v.wait_ge(squares_done, TB)
            mean_square(stat[:, 0:4], stat[:, 4:8]).then_inc(meansq_done, 1)
            v.wait_ge(std_done, 1)
            v.reciprocal(stat[:, 12:16], stat[:, 8:12]).then_inc(inv_done, 1)
            v.wait_ge(inv_done, 1)
            for m in range(3):
                v.tensor_scalar(XH[:, m, :], XH[:, m, :], stat[:, 12 + m:13 + m], None, ALU.mult).then_inc(norm_done, 1)
            lo(1, 0)
            v.wait_ge(free[4], 1)
            for k in range(KD):
                v.wait_ge(aT_hi, k + 1)
                v.scalar_tensor_tensor(out=aTl[:, k, :], in0=PS[:, k % 4, :], scalar=g1T[:, k:k + 1],
                                       in1=aTh[:, k, :].bitcast(F32), op0=ALU.mult, op1=ALU.subtract)\
                 .then_inc(free[k % 4], 1)

            def conv(g, a, b):
                def one(ap):
                    return ap.rearrange("p a t -> p (a t)")
                for n in range(a, b):
                    k, j = n // 2, n % 2
                    tap, c = TAPS - 1 - k, bass.ds(g * 2 + j, 1)
                    src, w = one(uT[:, c, tap:tap + T]), cwT[:, tap, c]
                    if k == 0:
                        v.wait_ge(glu_done, g * 2 + (j + 1))
                    v.wait_ge(conv_step, g * (2 * TAPS) + max(n, 1))
                    if k == 0:
                        v.tensor_scalar(acc[:, j, :], src, w, cbT[:, c], ALU.mult, ALU.add).then_inc(conv_step, 1)
                    else:
                        v.scalar_tensor_tensor(out=one(uT[:, c, 0:T]) if k == TAPS - 1 else acc[:, j, :], in0=src,
                                               scalar=w, in1=acc[:, j, :], op0=ALU.mult, op1=ALU.add)\
                         .then_inc(conv_step, 1)

            v.memset(uT[:, :, 0:PAD], 0.0).then_inc(conv_step, 1)
            for n in range(U_GLU):
                lo(n + 2, (n + 1) % 2)
            v.wait_ge(consts_loaded, 16 * 8)

            def glu_attn(g, first, base):
                lo_ = P if first else 0
                steps = Steps(attn_step, base)

                def score(hg):
                    b = hg % 2
                    s_max, s_neg, _, s_sub, _, _ = (soft[:, b, j, :] for j in range(6))
                    if not (first and hg < 2):
                        v.wait_ge(full[7], g * 4 + (FULL["attn"][7] + hg - 1))
                    for i in range(HG):
                        bank, at = 4 + i % 2, (i // 2) * 2 * P
                        if i < 2:
                            v.wait_ge(full[bank], g * 4 + (FULL["attn"][bank] + hg + 1))
                        ins = v.scalar_tensor_tensor(out=Sc[:, b, i, lo_:], in0=negdist[:, lo_:],
                                                     scalar=SLOPES[HG * hg + i], in1=PS[:, bank, at + lo_:at + 2 * P],
                                                     op0=ALU.mult, op1=ALU.add)
                        if i >= 2:
                            ins.then_inc(free[bank], 1)
                        else:
                            steps.did(ins)
                    for bank in (4, 5):
                        v.wait_ge(free[bank], g * 4 + (FREE["attn"][bank] + hg + 1))
                    steps.wait()
                    steps.did(v.tensor_reduce(s_max, Sc[:, b, :, lo_:], AX.X, ALU.max))
                    steps.wait()
                    steps.did(v.tensor_tensor(s_max, s_max, sinks[:, HG * hg:HG * (hg + 1)], ALU.max))
                    steps.wait()
                    steps.did(v.tensor_scalar(s_neg, s_max, -1.0, None, ALU.mult))
                    v.tensor_tensor(s_sub, sinks[:, HG * hg:HG * (hg + 1)], s_max, ALU.subtract)\
                     .then_inc(negmax_ready, 1)

                def norm(hg):
                    b = hg % 2
                    s_sum, s_exp, s_inv = soft[:, b, 2, :], soft[:, b, 4, :], soft[:, b, 5, :]
                    v.wait_ge(exp_done, g * 4 + (hg + 1))
                    steps.did(v.tensor_tensor(s_inv, s_sum, s_exp, ALU.add))
                    steps.wait()
                    steps.did(v.reciprocal(s_inv, s_inv))
                    steps.wait()
                    v.tensor_tensor(Sc[:, b, :, lo_:], Sc[:, b, :, lo_:],
                                    s_inv.unsqueeze(2).to_broadcast([P, HG, 2 * P - lo_]), ALU.mult).then_inc(p_ready, 1)

                def glu_lo(u):
                    lo(g * 4 + (U_GLU + u + 1), u % 2)

                glu_lo(1)
                score(0)
                score(1)
                glu_lo(2)
                norm(0)
                norm(1)
                score(2)
                glu_lo(3)
                norm(2)
                score(3)
                glu_lo(4)
                norm(3)
                v.wait_ge(halves, g * 8 + 2 * (U_GLU + 4))
                for b in range(2):
                    v.wait_ge(free[b], g + (FREE["glu"][b] + 1))
                    v.tensor_tensor(uT[:, bass.ds(g * 2 + b, 1), PAD:].rearrange("p a t -> p (a t)"),
                                    PS[:, 2 + b, :], glusig[:, b, :], ALU.mult).then_inc(free[2 + b], 1)
                for b in range(2):
                    v.wait_ge(free[2 + b], g + (FREE["glu"][2 + b] + 1))
                    v.sem_inc(glu_done, 1)
                return steps.n

            per_block = glu_attn(0, True, 0)
            with v.Fori(1, TB) as g:
                glu_attn(g, False, g * per_block)

            for n, (k0, view) in enumerate(OT_hi):
                chunks = slice(k0, k0 + view.shape[1])
                v.wait_ge(out_hi, n + 1)
                v.tensor_tensor(OT_lo[:, chunks, :], OT[:, chunks, :], view.bitcast(F32), ALU.subtract)\
                 .then_inc(out_lo, 1)

            def mix_to_aT(k):
                v.wait_ge(aT_hi, KD + k + 1)
                v.tensor_tensor(aTl[:, 4 * k:4 * k + 4, :], mixT[:, 4 * k:4 * k + 4, :],
                                aTh[:, 4 * k:4 * k + 4, :].bitcast(F32), ALU.subtract).then_inc(aT_lo, 1)

            def mix(branch, g, phase, ln, last):
                n0 = U_MIX + 6 * MIX_IT * branch

                def products(j0):
                    v.wait_ge(halves, g * 12 + 2 * (n0 + 5 + j0 // 2))
                    for j in (j0, j0 + 1):
                        v.wait_ge(free[j], g + (FREE[phase][j] + 1))
                        v.tensor_tensor(sig[:, j, :], PS[:, 4 + j, :], sig[:, j, :], ALU.mult).then_inc(free[4 + j], 1)
                    for j in (j0, j0 + 1):
                        v.wait_ge(free[4 + j], g + (FREE[phase][4 + j] + 1))
                        chunk = mixT[:, bass.ds(g * 4 + j, 1), :].rearrange("p a t -> p (a t)")
                        if branch == 0:
                            v.tensor_copy(chunk, sig[:, j, :]).then_inc(mix_ready, 1)
                        else:
                            v.tensor_tensor(chunk, chunk, sig[:, j, :], ALU.add).then_inc(mix_ready, 1)

                for u in range(1, 7):
                    if u == 6:
                        products(0)
                    lo(g * 6 + (n0 + u + 1), u % 2)
                    if branch == 0:
                        conv(g, CONV_AT[u - 1], CONV_AT[u])
                    if ln and u == 1:
                        v.wait_ge(conv_step, 1 + CC * TAPS)
                        sums = Steps(sum_step)
                        for c in range(1, CC):
                            if c > 1:
                                sums.wait()
                            sums.did(v.tensor_tensor(usum, uT[:, 0, 0:T] if c == 1 else usum, uT[:, c, 0:T], ALU.add))
                        v.wait_ge(free[4], FREE["ln"][4] + 1)
                        for c in range(CC):
                            v.tensor_tensor(uT[:, c, 0:T], uT[:, c, 0:T], mu, ALU.subtract).then_inc(centred, 1)
                    if ln and u == 2:
                        v.wait_ge(sq_used, CC)
                        v.tensor_scalar(rstd, PS[:, 5, :], LN_EPS, None, ALU.add).then_inc(free[5], 1)
                    if ln and u == 3:
                        v.wait_ge(lnstd_done, 1)
                        steps = Steps(ln_step)
                        steps.did(v.reciprocal(rstd, rstd))
                        steps.wait()
                        for c in range(CC):
                            steps.did(v.tensor_tensor(uT[:, c, 0:T], uT[:, c, 0:T], rstd, ALU.mult))
                    if ln and u == 4:
                        for c in range(CC):
                            v.wait_ge(out_hi, len(OT_hi) + c + 1)
                            v.tensor_tensor(uT_lo[:, c, 0:T], uT[:, c, 0:T], uT_hi[:, c, :].bitcast(F32),
                                            ALU.subtract).then_inc(out_lo, 1)
                    if last and u == 5:
                        for k in range(3):
                            mix_to_aT(k)
                products(2)

            with v.Fori(0, MIX_IT) as g:
                mix(0, g, "mixA", False, False)
            mix(1, 0, "mixB", True, False)
            with v.Fori(1, MIX_IT - 1) as g:
                mix(1, g, "mixB", False, False)
            mix(1, MIX_IT - 1, "mixB", False, True)
            mix_to_aT(3)

            with v.Fori(0, 4) as it:
                for u in range(4):
                    lo(it * 4 + (U_OUT + u + 2), (u + 1) % 2)
                    if u % 2:
                        v.wait_ge(x_reloaded, 16)
                        v.wait_ge(halves, it * 8 + 2 * (U_OUT + u + 1))
                        for m in range(TB):
                            bank = 4 * (u // 2) + m
                            h = XH[:, m, bass.ds(it * 2 * UC + (u // 2) * UC, UC)]
                            v.tensor_tensor(h, PS[:, bank, 0:UC], h, ALU.add).then_inc(free[bank], 1)

            for k in range(KD):
                v.wait_ge(aT_hi, KD + 4 + k + 1)
                v.scalar_tensor_tensor(out=aTl[:, k, :], in0=PS[:, k % 4, :], scalar=g2T[:, k:k + 1],
                                       in1=aTh[:, k, :].bitcast(F32), op0=ALU.mult, op1=ALU.subtract)\
                 .then_inc(free[k % 4], 1)
            lo(U_PQ + 2, 1)
            v.wait_ge(squares_done, 2 * TB)
            mean_square(stat[:, 0:4], stat[:, 4:8]).then_inc(meansq_done, 1)
            v.wait_ge(std_done, 2)
            v.reciprocal(stat[:, 12:16], stat[:, 8:12]).then_inc(inv_done, 1)
            v.wait_ge(inv_done, 2)

            def rank(it, j, blocks=range(TB), base=None):
                bank = 4 + j
                i = it * 4 + j
                b0, b1 = blocks[0], blocks[-1] + 1
                steps = Steps(rank_step, it * (4 * RANK_STEPS) + RANK_STEPS * j if base is None else base)
                v.wait_ge(full[bank], it + (FULL["pq"][bank] + 1))
                v.nop(nofuse=True)

                def src(m):
                    return PS[:, bank, m * NK:(m + 1) * NK]

                for m in blocks:
                    steps.did(v.max(bestv[:, m, 0:8], src(m)))
                steps.wait()
                for m in blocks:
                    steps.did(v.max_index(besti[:, m, 0:8], bestv[:, m, 0:8], src(m)))
                for m in blocks:
                    steps.did(v.match_replace(sc[:, m, :], bestv[:, m, 0:8], src(m), MASKED))
                steps.wait()
                v.sem_inc(free[bank], 1)
                for m in blocks:
                    steps.did(v.max(bestv[:, m, 8:16], sc[:, m, :]))
                steps.wait()
                for m in blocks:
                    steps.did(v.max_index(besti[:, m, 8:16], bestv[:, m, 8:16], sc[:, m, :]))
                steps.wait()
                steps.did(v.tensor_tensor(topv[:, b0:b1, bass.ds(i, 1), :].rearrange("p m a k -> p m (a k)"), bestv[:, b0:b1, :],
                                          stat[:, 12 + b0:12 + b1].unsqueeze(2).to_broadcast([P, b1 - b0, TOPK]), ALU.mult))
                steps.did(v.tensor_copy(topi[:, b0:b1, bass.ds(i, 1), :].rearrange("p m a k -> p m (a k)"), besti[:, b0:b1, :]))
                steps.wait()
                return steps.base + steps.n

            def choose(m, h):
                steps = Steps(head_step, m * (PH * HEAD_STEPS) + h * HEAD_STEPS)
                one, two = bass.ds(m, 1), bass.ds(h * 2, 2)
                tv, ti = (t[:, one, two, :].rearrange("p a s k -> p (a s) k") for t in (topv, topi))
                steps.did(v.tensor_tensor(cand, tv[:, 0, :].unsqueeze(2).to_broadcast([P, TOPK, TOPK]),
                                          tv[:, 1, :].unsqueeze(1).to_broadcast([P, TOPK, TOPK]), ALU.add))
                steps.wait()
                sums = cand.rearrange("p a b -> p (a b)")
                steps.did(v.max(sumv[:, 0:8], sums))
                steps.wait()
                steps.did(v.max_index(sumi[:, 0:8], sumv[:, 0:8], sums))
                steps.did(v.match_replace(cand2, sumv[:, 0:8], sums, MASKED))
                steps.wait()
                steps.did(v.max(sumv[:, 8:16], cand2))
                steps.wait()
                steps.did(v.max_index(sumi[:, 8:16], sumv[:, 8:16], cand2))
                steps.did(v.tensor_copy(tops[:, bass.ds(h, 1), :].rearrange("p a k -> p (a k)"), sumv))
                steps.wait()
                steps.did(v.tensor_scalar(sump[:, 0, :], sumi, 4, None, ALU.logical_shift_right))
                steps.did(v.tensor_scalar(sump[:, 1, :], sumi, TOPK - 1, None, ALU.bitwise_and))
                steps.wait()
                steps.did(v.tensor_copy(sumf, sump))
                steps.wait()
                steps.did(v.tensor_tensor(pick, sumf.unsqueeze(3).to_broadcast([P, 2, TOPK, TOPK]),
                                          iota16[:, :].unsqueeze(1).unsqueeze(1).to_broadcast([P, 2, TOPK, TOPK]), ALU.is_equal))
                steps.wait()
                steps.did(v.tensor_tensor(pick, pick, ti.unsqueeze(2).to_broadcast([P, 2, TOPK, TOPK]), ALU.mult))
                steps.wait()
                steps.did(v.tensor_reduce(isel, pick, AX.X, ALU.add))
                steps.wait()
                steps.did(v.scalar_tensor_tensor(out=idx[:, one, bass.ds(h * TOPK, TOPK)].rearrange("p a k -> p (a k)"),
                                                 in0=isel[:, 0, :], scalar=float(NK), in1=isel[:, 1, :],
                                                 op0=ALU.mult, op1=ALU.add))
                steps.wait()
                v.sem_inc(idx_ready, 1)
                assert steps.n == HEAD_STEPS

            def gate_shift(m):
                steps = Steps(gate_step, m * 4)
                steps.did(v.tensor_copy(rs[:, 0, :], tops[:, :, 0]))
                steps.wait()
                v.tensor_tensor(tops, tops, rs[:, 0, :].unsqueeze(2).to_broadcast([P, PH, TOPK]),
                                ALU.subtract).then_inc(sub_ready, 1)

            def gate_norm(m):
                steps = Steps(gate_step, m * 4 + 1)
                v.wait_ge(gexp_done, m + 1)
                steps.did(v.tensor_reduce(rs[:, 0, :], tops, AX.X, ALU.add))
                steps.wait()
                steps.did(v.reciprocal(rs[:, 1, :], rs[:, 0, :]))
                steps.wait()
                steps.did(v.tensor_tensor(gates[:, :].rearrange("p (h k) -> p h k", h=PH), tops,
                                          rs[:, 1, :].unsqueeze(2).to_broadcast([P, PH, TOPK]), ALU.mult))
                steps.wait()

            def peer_q(it, first, last):
                for u in range(4):
                    if not (first and u == 0 or last and u == 3):
                        lo(it * 4 + (U_PQ + u + 2), (u + 1) % 2)
                    if not first:
                        if u == 0:
                            choose(0, it * 2 - 2)
                        if u == 1:
                            rank(it - 1, 2)
                            rank(it - 1, 3)
                        if u == 2:
                            choose(0, it * 2 - 1)
                    if u == 3 and not last:
                        rank(it, 0)
                        rank(it, 1)

            peer_q(0, True, False)
            with v.Fori(1, 3) as it:
                peer_q(it, False, False)
            peer_q(3, False, True)
            ranked = RANK_STEPS * 4 * 3
            for h in (0, 1):
                for j in (2 * h, 2 * h + 1):
                    ranked = rank(3, j, range(1), ranked)
                choose(0, PH - 2 + h)
            v.sem_inc(tile_used, RING)

            def xn_to_psum(m):
                v.scalar_tensor_tensor(out=xn_ps, in0=XH[:, bass.ds(m, 1), :].rearrange("p a n -> p (a n)"),
                                       scalar=stat[:, bass.ds(m + 12, 1)], in1=g2b, op0=ALU.mult, op1=ALU.mult)\
                 .then_inc(xn_in_psum, 1)

            def add_v(m, r, tiles):
                for n in range(tiles):
                    s = n % RING
                    v.wait_ge(gathered[s], m * (32 * (HK // RING)) + r * (2 * tiles) + 16 * (HK // RING + 1 + n // RING))
                    v.wait_ge(tile_used, m * 2 * HK + r * tiles + (RING + HK + n))
                    v.scalar_tensor_tensor(out=y_ps, in0=ring[:, s, :], scalar=hact[:, bass.ds(r * tiles + n, 1)],
                                           in1=y_ps, op0=ALU.mult, op1=ALU.add).then_inc(tile_used, 1)

            def experts(m, last):
                v.wait_ge(xn_in_psum, m + 1)
                v.nop(nofuse=True)
                with v.Fori(0, HK // RING) as r:
                    for s in range(RING):
                        v.wait_ge(gathered[s], m * (32 * (HK // RING)) + r * 16 + 16)
                        v.scalar_tensor_tensor(out=ring[:, s, :], in0=ring[:, s, :], scalar=1.0, in1=xn_ps,
                                               op0=ALU.mult, op1=ALU.mult,
                                               accum_out=hid[:, bass.ds(r * RING + s, 1)]).then_inc(tile_used, 1)
                v.wait_ge(tile_used, m * 2 * HK + (RING + HK))
                v.memset(y_ps, 0.0).then_inc(y_cleared, 1)
                gate_norm(m)
                v.wait_ge(gelu_done, m + 1)
                v.tensor_tensor(hact[:, :], hact[:, :], gates[:, :], ALU.mult).then_inc(hact_ready, 1)
                if not last:
                    xn_to_psum(m + 1)
                v.wait_ge(y_cleared, m + 1)
                v.wait_ge(hact_ready, m + 1)
                v.nop(nofuse=True)
                with v.Fori(0, PH) as h:
                    if not last:
                        choose(m + 1, h)
                    add_v(m, h, HK // PH)
                if not last:
                    gate_shift(m + 1)
                v.wait_ge(tile_used, m * 2 * HK + (RING + 2 * HK))
                hm = XH[:, bass.ds(m, 1), :].rearrange("p a n -> p (a n)")
                v.tensor_tensor(hm, y_ps, hm, ALU.add).then_inc(y_added, 1)
                v.wait_ge(fin_sq, m + 1)
                mean_square(stat[:, 0:1], stat[:, 1:2]).then_inc(fin_ms, 1)
                v.wait_ge(fin_std, m + 1)
                v.reciprocal(stat[:, 3:4], stat[:, 2:3]).then_inc(fin_step, 1)
                v.wait_ge(fin_step, m + 1)
                v.scalar_tensor_tensor(out=hm, in0=hm, scalar=stat[:, 3:4], in1=gfin, op0=ALU.mult,
                                       op1=ALU.mult).then_inc(out_ready, 1)

            v.wait_ge(keys_loaded, 16 * 3)
            xn_to_psum(0)
            gate_shift(0)
            for j in range(4):
                ranked = rank(3, j, range(1, TB), ranked)
            with v.Fori(0, TB - 1) as m:
                experts(m, False)
            experts(TB - 1, True)

    return nc


_INS = ["x", "norm_mix_g", "w_in", "conv_dw_w", "conv_dw_b", "conv_ln_g", "conv_ln_b", "w_conv_out", "attn_sinks",
        "w_attn_out", "w_out", "norm_ffn_g", "peer_w_q", "peer_sub_keys", "peer_u", "peer_v", "final_norm_g"]


def kernel(**inputs):
    import concourse.bacc as bacc
    from concourse.bass_utils import run_bass_kernel_spmd

    nc = bacc.Bacc("TRN2", target_bir_lowering=False, num_devices=1)
    arrays, args = {}, []
    for name in _INS:
        a = np.ascontiguousarray(inputs[name])
        arrays[f"in_{name}"] = a
        args.append(nc.dram_tensor(f"in_{name}", a.shape, mybir.dt.from_np(a.dtype), kind="ExternalInput").ap())
    shape = arrays["in_x"].shape
    args.append(nc.dram_tensor("out_h", shape, F32, kind="ExternalOutput").ap())
    build(nc, *args)
    r = run_bass_kernel_spmd(nc, [arrays], core_ids=[0])
    return r.results[0]["out_h"]
```
